# Optimizing a Trainium2 kernel written in Bass

```python
import math
import jax, jax.numpy as jnp
from jax import lax
import numpy as np

D_MODEL = 1024
BATCH = 1
SEQ = 256
DEPTH = 2

MIX_WIDTH = D_MODEL
HEAD_DIM = 64
ATTN_WIDTH = D_MODEL // 2
N_Q_HEADS = ATTN_WIDTH // HEAD_DIM
N_KV_HEADS = N_Q_HEADS // 4
KV_WIDTH = N_KV_HEADS * HEAD_DIM
WINDOW = 128
BLOCK = 128
ROPE_THETA = 500000.0
ROPE_DIM = HEAD_DIM // 4
CONV_WIDTH = D_MODEL // 4
CONV_K = 3
POOL_WIDTH = D_MODEL // 4
POOL_WINDOWS = (2, 4, 8, 16)
POOL_GROUP = POOL_WIDTH // len(POOL_WINDOWS)
IN_WIDTH = ATTN_WIDTH + 2 * KV_WIDTH + 3 * CONV_WIDTH + POOL_WIDTH
IN_SPLITS = (ATTN_WIDTH,
             ATTN_WIDTH + KV_WIDTH,
             ATTN_WIDTH + 2 * KV_WIDTH,
             ATTN_WIDTH + 2 * KV_WIDTH + CONV_WIDTH,
             ATTN_WIDTH + 2 * KV_WIDTH + 2 * CONV_WIDTH,
             ATTN_WIDTH + 2 * KV_WIDTH + 3 * CONV_WIDTH)
PEER_HEADS = 8
PEER_NKEYS = 128
PEER_EXPERTS = PEER_NKEYS * PEER_NKEYS
PEER_QDIM = 256
PEER_TOPK = 16
PEER_CHUNK = 128
EPS = 1e-6
MASK_VALUE = -1e30


def rms_norm(t, g):
    tf = t.astype(jnp.float32)
    y = tf * lax.rsqrt(jnp.mean(tf * tf, axis=-1, keepdims=True) + EPS)
    return (y * g.astype(jnp.float32)).astype(t.dtype)

def rope_tables(positions):
    inv = ROPE_THETA ** (-jnp.arange(0, ROPE_DIM, 2, dtype=jnp.float32) / ROPE_DIM)
    ang = positions.astype(jnp.float32)[..., None] * inv
    return jnp.cos(ang)[:, :, None, :], jnp.sin(ang)[:, :, None, :]

def partial_rope(t, cos, sin):
    half = ROPE_DIM // 2
    t1 = t[..., :half].astype(jnp.float32)
    t2 = t[..., half:ROPE_DIM].astype(jnp.float32)
    rot = jnp.concatenate([t1 * cos - t2 * sin, t2 * cos + t1 * sin], axis=-1).astype(t.dtype)
    return jnp.concatenate([rot, t[..., ROPE_DIM:]], axis=-1)

def windowed_gqa(q, k, v, sink):
    b, s = q.shape[0], q.shape[1]
    nb = s // BLOCK
    grp = N_Q_HEADS // N_KV_HEADS
    qb = q.reshape(b, nb, BLOCK, N_KV_HEADS, grp, HEAD_DIM)

    def bands(t):
        tp = jnp.pad(t, ((0, 0), (BLOCK, BLOCK), (0, 0), (0, 0)))
        tp = tp.reshape(b, nb + 2, BLOCK, N_KV_HEADS, HEAD_DIM)
        return jnp.concatenate([tp[:, :-2], tp[:, 1:-1], tp[:, 2:]], axis=2)

    kb, vb = bands(k), bands(v)
    scores = jnp.einsum('bnqhgd,bnkhd->bnhgqk', qb, kb).astype(jnp.float32) * (HEAD_DIM ** -0.5)
    qpos = jnp.arange(s).reshape(nb, BLOCK, 1)
    kpos = (jnp.arange(nb)[:, None, None] - 1) * BLOCK + jnp.arange(3 * BLOCK)[None, None, :]
    valid = (jnp.abs(qpos - kpos) <= WINDOW) & (kpos >= 0) & (kpos < s)
    scores = jnp.where(valid[None, :, None, None], scores, MASK_VALUE)
    sink_col = jnp.broadcast_to(
        sink.astype(jnp.float32).reshape(1, 1, N_KV_HEADS, grp, 1, 1), scores.shape[:-1] + (1,))
    probs = jax.nn.softmax(jnp.concatenate([scores, sink_col], axis=-1), axis=-1)[..., :-1]
    out = jnp.einsum('bnhgqk,bnkhd->bnqhgd', probs.astype(v.dtype), vb)
    return out.reshape(b, s, N_Q_HEADS * HEAD_DIM)

def short_conv(u, w):
    up = jnp.pad(u, ((0, 0), (1, 1), (0, 0)))
    return w[0] * up[:, :-2] + w[1] * up[:, 1:-1] + w[2] * up[:, 2:]

def multiscale_pool(u):
    s = u.shape[1]
    t = jnp.arange(s)
    uf = u.astype(jnp.float32)
    cs = jnp.pad(jnp.cumsum(uf, axis=1), ((0, 0), (1, 0), (0, 0)))
    outs = []
    for gi, w in enumerate(POOL_WINDOWS):
        lo = jnp.clip(t - w // 2, 0, s)
        hi = jnp.clip(t + w // 2, 0, s)
        csg = cs[..., gi * POOL_GROUP:(gi + 1) * POOL_GROUP]
        cnt = (hi - lo).astype(jnp.float32)[None, :, None]
        mean = (jnp.take(csg, hi, axis=1) - jnp.take(csg, lo, axis=1)) / cnt
        outs.append(mean - uf[..., gi * POOL_GROUP:(gi + 1) * POOL_GROUP])
    return jnp.stack(outs, axis=2).astype(u.dtype)

def peer_ffn(h, w_q, sub_keys, expert_u, expert_v):
    b, s, d = h.shape
    n_tok = b * s
    ht = h.reshape(n_tok, d)
    q = (ht @ w_q).reshape(n_tok, PEER_HEADS, PEER_QDIM)
    half = PEER_QDIM // 2
    s1 = jnp.einsum('thd,kd->thk', q[..., :half], sub_keys[0]).astype(jnp.float32)
    s2 = jnp.einsum('thd,kd->thk', q[..., half:], sub_keys[1]).astype(jnp.float32)
    v1, i1 = lax.top_k(s1, PEER_TOPK)
    v2, i2 = lax.top_k(s2, PEER_TOPK)
    cand = (v1[..., :, None] + v2[..., None, :]).reshape(n_tok, PEER_HEADS, PEER_TOPK * PEER_TOPK)
    cidx = (i1[..., :, None] * PEER_NKEYS + i2[..., None, :]).reshape(n_tok, PEER_HEADS, PEER_TOPK * PEER_TOPK)
    top, pos = lax.top_k(cand, PEER_TOPK)
    eidx = jnp.take_along_axis(cidx, pos, axis=-1)
    gate = jax.nn.softmax(top, axis=-1).astype(h.dtype)
    n_chunks = n_tok // PEER_CHUNK

    def chunk(args):
        hc, ec, gc = args
        u = expert_u[ec]
        act = jax.nn.gelu(jnp.einsum('td,thkd->thk', hc, u), approximate=False)
        return jnp.einsum('thk,thkd->td', gc * act, expert_v[ec])

    y = lax.map(chunk, (ht.reshape(n_chunks, PEER_CHUNK, d),
                        eidx.reshape(n_chunks, PEER_CHUNK, PEER_HEADS, PEER_TOPK),
                        gate.reshape(n_chunks, PEER_CHUNK, PEER_HEADS, PEER_TOPK)))
    return y.reshape(b, s, d)

def first_inputs(seed: int = 0) -> dict:
    key = jax.random.key(seed)
    ks = jax.random.split(key, 20)
    L, D = DEPTH, D_MODEL

    def nrm(k, shape, scale):
        return jax.random.normal(k, shape, jnp.float32) * scale

    return {
        "x": nrm(ks[0], (BATCH, SEQ, D), 1.0),
        "c": nrm(ks[1], (BATCH, D), 1.0),
        "positions": jnp.arange(SEQ, dtype=jnp.int32)[None, :]
                     + jax.random.randint(ks[2], (BATCH, 1), 0, 1024, dtype=jnp.int32),
        "norm1_g": 1.0 + nrm(ks[3], (L, D), 0.02),
        "norm2_g": 1.0 + nrm(ks[4], (L, D), 0.02),
        "w_ada": nrm(ks[5], (L, D, 6 * D), 0.5 * D ** -0.5),
        "b_ada": nrm(ks[6], (L, 6 * D), 0.02),
        "w_in": nrm(ks[7], (L, D, IN_WIDTH), D ** -0.5),
        "q_norm_g": 1.0 + nrm(ks[8], (L, HEAD_DIM), 0.02),
        "k_norm_g": 1.0 + nrm(ks[9], (L, HEAD_DIM), 0.02),
        "attn_sink": nrm(ks[10], (L, N_Q_HEADS), 0.5),
        "conv_w": nrm(ks[11], (L, CONV_K, CONV_WIDTH), CONV_K ** -0.5),
        "pool_w": nrm(ks[12], (L, len(POOL_WINDOWS), POOL_GROUP, POOL_GROUP), POOL_GROUP ** -0.5),
        "pool_scale": 1.0 + nrm(ks[13], (L, POOL_WIDTH), 0.1),
        "w_out": nrm(ks[14], (L, MIX_WIDTH, D), MIX_WIDTH ** -0.5),
        "peer_wq": nrm(ks[15], (L, D, PEER_HEADS * PEER_QDIM), D ** -0.5),
        "peer_keys": nrm(ks[16], (L, 2, PEER_NKEYS, PEER_QDIM // 2), (PEER_QDIM // 2) ** -0.5),
        "peer_u": nrm(ks[17], (L, PEER_EXPERTS, D), D ** -0.5),
        "peer_v": nrm(ks[18], (L, PEER_EXPERTS, D), PEER_HEADS ** -0.5),
    }

def first_block(x, c, positions, norm1_g, norm2_g, w_ada, b_ada, w_in, q_norm_g, k_norm_g,
              attn_sink, conv_w, pool_w, pool_scale, w_out, peer_wq, peer_keys, peer_u, peer_v):
    b, s, d = x.shape
    cos, sin = rope_tables(positions)
    c_act = jax.nn.silu(c)
    for l in range(DEPTH):
        mod = (c_act @ w_ada[l] + b_ada[l])[:, None, :]
        shift1, scale1, gate1, shift2, scale2, gate2 = jnp.split(mod, 6, axis=-1)

        h = rms_norm(x, norm1_g[l]) * (1.0 + scale1) + shift1
        z = h @ w_in[l]
        q, k, v, conv_x, conv_b, conv_c, pool_x = jnp.split(z, IN_SPLITS, axis=-1)

        q = q.reshape(b, s, N_Q_HEADS, HEAD_DIM)
        k = k.reshape(b, s, N_KV_HEADS, HEAD_DIM)
        v = v.reshape(b, s, N_KV_HEADS, HEAD_DIM)
        q = partial_rope(rms_norm(q, q_norm_g[l]), cos, sin)
        k = partial_rope(rms_norm(k, k_norm_g[l]), cos, sin)
        attn_o = windowed_gqa(q, k, v, attn_sink[l])

        conv_o = conv_b * short_conv(conv_c * conv_x, conv_w[l])

        pooled = multiscale_pool(pool_x)
        pool_o = jnp.einsum('bsgc,gce->bsge', pooled, pool_w[l]).reshape(b, s, POOL_WIDTH) * pool_scale[l]

        mix = jnp.concatenate([attn_o, conv_o, pool_o], axis=-1) @ w_out[l]
        x = x + gate1 * mix

        h2 = rms_norm(x, norm2_g[l]) * (1.0 + scale2) + shift2
        x = x + gate2 * peer_ffn(h2, peer_wq[l], peer_keys[l], peer_u[l], peer_v[l])
    return x


DEPTH_2 = 1

MIX_WIDTH_2 = D_MODEL
S5_WIDTH = D_MODEL // 4
S5_GROUP_DIM = 16
S5_GROUPS = S5_WIDTH // S5_GROUP_DIM
S5_STATE = 64
SSD_INNER = MIX_WIDTH_2 - S5_WIDTH
SSD_HEAD_DIM = 64
SSD_HEADS = SSD_INNER // SSD_HEAD_DIM
SSD_GROUPS = 4
SSD_HPG = SSD_HEADS // SSD_GROUPS
SSD_STATE = 128
SSD_CONV = 4
SSD_CHUNK = 128
SSD_CONV_DIM = SSD_INNER + 2 * SSD_GROUPS * SSD_STATE
IN_COLS = S5_WIDTH + SSD_INNER + SSD_CONV_DIM + SSD_HEADS
MEM_LEN = 256
XA_HEADS = 4
XA_HEAD_DIM = D_MODEL // XA_HEADS
D_FF = 256 * ((8 * D_MODEL // 3 + 255) // 256)
FFN_CONV = 3
NORM_EPS = 1e-6


def rmsnorm(x, w):
    xf = x.astype(jnp.float32)
    xf = xf * lax.rsqrt(jnp.mean(xf * xf, axis=-1, keepdims=True) + NORM_EPS)
    return (xf * w.astype(jnp.float32)).astype(x.dtype)

def causal_dwconv(x, w, b):
    k = w.shape[0]
    l = x.shape[1]
    xp = jnp.pad(x, ((0, 0), (k - 1, 0), (0, 0)))
    y = xp[:, 0:l] * w[0]
    for i in range(1, k):
        y = y + xp[:, i:i + l] * w[i]
    return y + b

def s5_mixer(u, lam_re, lam_im, log_dt, b_re, b_im, c_re, c_im, d_skip, w_glu):
    bsz, l, _ = u.shape
    f32 = jnp.float32
    uf = u.reshape(bsz, l, S5_GROUPS, S5_GROUP_DIM).astype(f32)
    lr = jnp.minimum(lam_re.astype(f32), -1e-4)
    li = lam_im.astype(f32)
    dt = jnp.exp(log_dt.astype(f32))[:, None]
    mag = jnp.exp(lr * dt)
    ab_re = mag * jnp.cos(li * dt)
    ab_im = mag * jnp.sin(li * dt)
    den = lr * lr + li * li
    f_re = ((ab_re - 1.0) * lr + ab_im * li) / den
    f_im = (ab_im * lr - (ab_re - 1.0) * li) / den
    br = b_re.astype(f32)
    bi = b_im.astype(f32)
    bb_re = f_re[..., None] * br - f_im[..., None] * bi
    bb_im = f_re[..., None] * bi + f_im[..., None] * br
    bu_re = jnp.einsum('blgc,gpc->blgp', uf, bb_re)
    bu_im = jnp.einsum('blgc,gpc->blgp', uf, bb_im)
    a_re = jnp.broadcast_to(ab_re, bu_re.shape)
    a_im = jnp.broadcast_to(ab_im, bu_im.shape)

    def combine(e1, e2):
        a1r, a1i, b1r, b1i = e1
        a2r, a2i, b2r, b2i = e2
        return (a2r * a1r - a2i * a1i,
                a2r * a1i + a2i * a1r,
                a2r * b1r - a2i * b1i + b2r,
                a2r * b1i + a2i * b1r + b2i)

    _, _, h_re, h_im = lax.associative_scan(combine, (a_re, a_im, bu_re, bu_im), axis=1)
    y = (jnp.einsum('blgp,gcp->blgc', h_re, c_re.astype(f32))
         - jnp.einsum('blgp,gcp->blgc', h_im, c_im.astype(f32)))
    y = y + uf * d_skip.astype(f32).reshape(S5_GROUPS, S5_GROUP_DIM)
    y = jax.nn.gelu(y.reshape(bsz, l, S5_WIDTH))
    y = y * jax.nn.sigmoid(y @ w_glu.astype(f32))
    return y.astype(u.dtype)

def ssd_mixer(z, xbc, dt_raw, conv_w, conv_b, dt_bias, a_log, d_skip, norm_w):
    bsz, l, _ = xbc.shape
    f32 = jnp.float32
    nc = l // SSD_CHUNK
    xbc = jax.nn.silu(causal_dwconv(xbc, conv_w, conv_b))
    xs = xbc[..., :SSD_INNER]
    bmat = xbc[..., SSD_INNER:SSD_INNER + SSD_GROUPS * SSD_STATE]
    cmat = xbc[..., SSD_INNER + SSD_GROUPS * SSD_STATE:]
    x = xs.reshape(bsz, nc, SSD_CHUNK, SSD_GROUPS, SSD_HPG, SSD_HEAD_DIM)
    bm = bmat.reshape(bsz, nc, SSD_CHUNK, SSD_GROUPS, SSD_STATE)
    cm = cmat.reshape(bsz, nc, SSD_CHUNK, SSD_GROUPS, SSD_STATE)
    dt = jax.nn.softplus(dt_raw.astype(f32) + dt_bias.astype(f32))
    a = -jnp.exp(a_log.astype(f32))
    dt_c = dt.reshape(bsz, nc, SSD_CHUNK, SSD_GROUPS, SSD_HPG)
    da = jnp.moveaxis(dt_c * a.reshape(SSD_GROUPS, SSD_HPG), 2, -1)
    a_cs = jnp.cumsum(da, axis=-1)
    xdt = x.astype(f32) * dt_c[..., None]
    seg = a_cs[..., :, None] - a_cs[..., None, :]
    causal = jnp.tril(jnp.ones((SSD_CHUNK, SSD_CHUNK), dtype=bool))
    lmat = jnp.exp(jnp.where(causal, seg, -jnp.inf))
    cb = jnp.einsum('bclgn,bcsgn->bcgls', cm.astype(f32), bm.astype(f32))
    y_diag = jnp.einsum('bcgls,bcghls,bcsghp->bclghp', cb, lmat, xdt)
    decay_states = jnp.exp(a_cs[..., -1:] - a_cs)
    states = jnp.einsum('bclgn,bcghl,bclghp->bcghpn', bm.astype(f32), decay_states, xdt)
    chunk_decay = jnp.exp(a_cs[..., -1])

    def step(carry, inp):
        st, dec = inp
        return carry * dec[..., None, None] + st, carry

    init = jnp.zeros((bsz, SSD_GROUPS, SSD_HPG, SSD_HEAD_DIM, SSD_STATE), f32)
    _, prev = lax.scan(step, init, (jnp.moveaxis(states, 1, 0), jnp.moveaxis(chunk_decay, 1, 0)))
    prev = jnp.moveaxis(prev, 0, 1)
    y_off = jnp.einsum('bclgn,bcghpn,bcghl->bclghp', cm.astype(f32), prev, jnp.exp(a_cs))
    y = y_diag + y_off + x.astype(f32) * d_skip.astype(f32).reshape(SSD_GROUPS, SSD_HPG)[:, :, None]
    y = y.reshape(bsz, l, SSD_INNER).astype(z.dtype)
    return rmsnorm(y * jax.nn.silu(z), norm_w)

def cross_attention(h, mem_n, wq, wk, wv, wo):
    bsz, l, _ = h.shape
    m = mem_n.shape[1]
    q = (h @ wq).reshape(bsz, l, XA_HEADS, XA_HEAD_DIM)
    k = (mem_n @ wk).reshape(bsz, m, XA_HEADS, XA_HEAD_DIM)
    v = (mem_n @ wv).reshape(bsz, m, XA_HEADS, XA_HEAD_DIM)
    s = jnp.einsum('blhd,bmhd->bhlm', q, k).astype(jnp.float32) * (XA_HEAD_DIM ** -0.5)
    p = jax.nn.softmax(s, axis=-1).astype(v.dtype)
    o = jnp.einsum('bhlm,bmhd->blhd', p, v).reshape(bsz, l, D_MODEL)
    return o @ wo

def conv_ffn(h, w_up, conv_w, conv_b, w_down):
    gv = h @ w_up
    g = causal_dwconv(gv[..., :D_FF], conv_w, conv_b)
    v = gv[..., D_FF:]
    return (jax.nn.silu(g) * v) @ w_down

def second_inputs(seed: int = 0) -> dict:
    key = jax.random.key(seed)
    ks = jax.random.split(key, 32)
    f32 = jnp.float32

    def nrm(k, shape, scale):
        return jax.random.normal(k, shape, f32) * scale

    def gain(k, shape):
        return 1.0 + 0.02 * jax.random.normal(k, shape, f32)

    L = DEPTH_2
    x = jax.random.normal(ks[0], (BATCH, SEQ, D_MODEL), f32)
    mem = jax.random.normal(ks[1], (BATCH, MEM_LEN, D_MODEL), f32)
    mix_norm_w = gain(ks[2], (L, D_MODEL))
    w_in = nrm(ks[3], (L, D_MODEL, IN_COLS), D_MODEL ** -0.5)
    n_idx = jnp.arange(S5_STATE, dtype=f32)
    s5_lambda_re = -0.5 + 0.01 * jax.random.normal(ks[4], (L, S5_GROUPS, S5_STATE), f32)
    s5_lambda_im = math.pi * n_idx + 0.01 * jax.random.normal(ks[5], (L, S5_GROUPS, S5_STATE), f32)
    s5_log_dt = jax.random.uniform(ks[6], (L, S5_GROUPS), f32, math.log(0.001), math.log(0.1))
    s5_b_re = nrm(ks[7], (L, S5_GROUPS, S5_STATE, S5_GROUP_DIM), (2 * S5_GROUP_DIM) ** -0.5)
    s5_b_im = nrm(ks[8], (L, S5_GROUPS, S5_STATE, S5_GROUP_DIM), (2 * S5_GROUP_DIM) ** -0.5)
    s5_c_re = nrm(ks[9], (L, S5_GROUPS, S5_GROUP_DIM, S5_STATE), S5_STATE ** -0.5)
    s5_c_im = nrm(ks[10], (L, S5_GROUPS, S5_GROUP_DIM, S5_STATE), S5_STATE ** -0.5)
    s5_d = nrm(ks[11], (L, S5_WIDTH), 1.0)
    s5_w_glu = nrm(ks[12], (L, S5_WIDTH, S5_WIDTH), S5_WIDTH ** -0.5)
    ssd_conv_w = nrm(ks[13], (L, SSD_CONV, SSD_CONV_DIM), SSD_CONV ** -0.5)
    ssd_conv_b = nrm(ks[14], (L, SSD_CONV_DIM), 0.01)
    dt0 = jnp.exp(jax.random.uniform(ks[15], (L, SSD_HEADS), f32, math.log(0.001), math.log(0.1)))
    ssd_dt_bias = dt0 + jnp.log(-jnp.expm1(-dt0))
    ssd_a_log = jnp.log(jax.random.uniform(ks[16], (L, SSD_HEADS), f32, 1.0, 16.0))
    ssd_d = gain(ks[17], (L, SSD_HEADS))
    ssd_norm_w = gain(ks[18], (L, SSD_INNER))
    w_out = nrm(ks[19], (L, MIX_WIDTH_2, D_MODEL), MIX_WIDTH_2 ** -0.5)
    xa_norm_w = gain(ks[20], (L, D_MODEL))
    mem_norm_w = gain(ks[21], (L, D_MODEL))
    xa_wq = nrm(ks[22], (L, D_MODEL, D_MODEL), D_MODEL ** -0.5)
    xa_wk = nrm(ks[23], (L, D_MODEL, D_MODEL), D_MODEL ** -0.5)
    xa_wv = nrm(ks[24], (L, D_MODEL, D_MODEL), D_MODEL ** -0.5)
    xa_wo = nrm(ks[25], (L, D_MODEL, D_MODEL), D_MODEL ** -0.5)
    ffn_norm_w = gain(ks[26], (L, D_MODEL))
    ffn_w_up = nrm(ks[27], (L, D_MODEL, 2 * D_FF), D_MODEL ** -0.5)
    ffn_conv_w = nrm(ks[28], (L, FFN_CONV, D_FF), FFN_CONV ** -0.5)
    ffn_conv_b = nrm(ks[29], (L, D_FF), 0.01)
    ffn_w_down = nrm(ks[30], (L, D_FF, D_MODEL), D_FF ** -0.5)
    final_norm_w = gain(ks[31], (D_MODEL,))
    return {"x": x, "mem": mem, "mix_norm_w": mix_norm_w, "w_in": w_in,
            "s5_lambda_re": s5_lambda_re, "s5_lambda_im": s5_lambda_im, "s5_log_dt": s5_log_dt,
            "s5_b_re": s5_b_re, "s5_b_im": s5_b_im, "s5_c_re": s5_c_re, "s5_c_im": s5_c_im,
            "s5_d": s5_d, "s5_w_glu": s5_w_glu,
            "ssd_conv_w": ssd_conv_w, "ssd_conv_b": ssd_conv_b, "ssd_dt_bias": ssd_dt_bias,
            "ssd_a_log": ssd_a_log, "ssd_d": ssd_d, "ssd_norm_w": ssd_norm_w, "w_out": w_out,
            "xa_norm_w": xa_norm_w, "mem_norm_w": mem_norm_w, "xa_wq": xa_wq, "xa_wk": xa_wk,
            "xa_wv": xa_wv, "xa_wo": xa_wo, "ffn_norm_w": ffn_norm_w, "ffn_w_up": ffn_w_up,
            "ffn_conv_w": ffn_conv_w, "ffn_conv_b": ffn_conv_b, "ffn_w_down": ffn_w_down,
            "final_norm_w": final_norm_w}

def second_block(x, mem, mix_norm_w, w_in, s5_lambda_re, s5_lambda_im, s5_log_dt, s5_b_re, s5_b_im,
              s5_c_re, s5_c_im, s5_d, s5_w_glu, ssd_conv_w, ssd_conv_b, ssd_dt_bias, ssd_a_log,
              ssd_d, ssd_norm_w, w_out, xa_norm_w, mem_norm_w, xa_wq, xa_wk, xa_wv, xa_wo,
              ffn_norm_w, ffn_w_up, ffn_conv_w, ffn_conv_b, ffn_w_down, final_norm_w):
    c_u = S5_WIDTH
    c_z = c_u + SSD_INNER
    c_xbc = c_z + SSD_CONV_DIM
    for i in range(DEPTH_2):
        h = rmsnorm(x, mix_norm_w[i])
        proj = h @ w_in[i]
        y_s5 = s5_mixer(proj[..., :c_u], s5_lambda_re[i], s5_lambda_im[i], s5_log_dt[i],
                        s5_b_re[i], s5_b_im[i], s5_c_re[i], s5_c_im[i], s5_d[i], s5_w_glu[i])
        y_ssd = ssd_mixer(proj[..., c_u:c_z], proj[..., c_z:c_xbc], proj[..., c_xbc:],
                          ssd_conv_w[i], ssd_conv_b[i], ssd_dt_bias[i], ssd_a_log[i],
                          ssd_d[i], ssd_norm_w[i])
        x = x + jnp.concatenate([y_s5, y_ssd], axis=-1) @ w_out[i]
        h = rmsnorm(x, xa_norm_w[i])
        mem_n = rmsnorm(mem, mem_norm_w[i])
        x = x + cross_attention(h, mem_n, xa_wq[i], xa_wk[i], xa_wv[i], xa_wo[i])
        h = rmsnorm(x, ffn_norm_w[i])
        x = x + conv_ffn(h, ffn_w_up[i], ffn_conv_w[i], ffn_conv_b[i], ffn_w_down[i])
    return rmsnorm(x, final_norm_w)


def setup_inputs(seed=0):
    out = dict(first_inputs(seed))
    for name, value in second_inputs(seed + 1).items():
        if name != "x":
            out[name + "_2"] = value
    return out


def reference(
    x, c, positions, norm1_g, norm2_g, w_ada, b_ada, w_in, q_norm_g, k_norm_g, attn_sink,
    conv_w, pool_w, pool_scale, w_out, peer_wq, peer_keys, peer_u, peer_v, mem_2, mix_norm_w_2,
    w_in_2, s5_lambda_re_2, s5_lambda_im_2, s5_log_dt_2, s5_b_re_2, s5_b_im_2, s5_c_re_2,
    s5_c_im_2, s5_d_2, s5_w_glu_2, ssd_conv_w_2, ssd_conv_b_2, ssd_dt_bias_2, ssd_a_log_2,
    ssd_d_2, ssd_norm_w_2, w_out_2, xa_norm_w_2, mem_norm_w_2, xa_wq_2, xa_wk_2, xa_wv_2,
    xa_wo_2, ffn_norm_w_2, ffn_w_up_2, ffn_conv_w_2, ffn_conv_b_2, ffn_w_down_2, final_norm_w_2,
):
    x = first_block(
        x, c, positions, norm1_g, norm2_g, w_ada, b_ada, w_in, q_norm_g, k_norm_g, attn_sink,
        conv_w, pool_w, pool_scale, w_out, peer_wq, peer_keys, peer_u, peer_v,
    )
    return second_block(
        x, mem_2, mix_norm_w_2, w_in_2, s5_lambda_re_2, s5_lambda_im_2, s5_log_dt_2, s5_b_re_2,
        s5_b_im_2, s5_c_re_2, s5_c_im_2, s5_d_2, s5_w_glu_2, ssd_conv_w_2, ssd_conv_b_2,
        ssd_dt_bias_2, ssd_a_log_2, ssd_d_2, ssd_norm_w_2, w_out_2, xa_norm_w_2, mem_norm_w_2,
        xa_wq_2, xa_wk_2, xa_wv_2, xa_wo_2, ffn_norm_w_2, ffn_w_up_2, ffn_conv_w_2,
        ffn_conv_b_2, ffn_w_down_2, final_norm_w_2,
    )


_drawn_inputs = setup_inputs


def setup_inputs(seed=0):
    import zlib

    import numpy as np

    out = dict(_drawn_inputs(seed))
    spreads = {}
    factors = {'norm1_g': 3.465,
     'norm2_g': 3.67,
     'q_norm_g': 8.0,
     'k_norm_g': 8.0,
     'attn_sink': 8.0,
     'mix_norm_w_2': 2.824,
     's5_lambda_re_2': 64.0,
     's5_lambda_im_2': 37.752,
     's5_log_dt_2': 38.032,
     's5_b_re_2': 52.384,
     's5_b_im_2': 52.056,
     's5_c_re_2': 54.224,
     's5_c_im_2': 52.008,
     'ssd_conv_b_2': 6.32,
     'ssd_d_2': 168.807,
     'ssd_norm_w_2': 4.289,
     'xa_norm_w_2': 8.0,
     'mem_norm_w_2': 8.0,
     'ffn_norm_w_2': 4.759,
     'ffn_conv_b_2': 33.946,
     'final_norm_w_2': 21.977}
    for name, (base, spread) in spreads.items():
        noise = np.random.default_rng([zlib.crc32(name.encode()), seed]).standard_normal(out[name].shape)
        drawn = base * np.exp(spread * noise) if base else spread * noise
        out[name] = __import__('jax').numpy.asarray(drawn.astype(out[name].dtype))
    for name, factor in factors.items():
        out[name] = (out[name] * factor).astype(out[name].dtype)
    return out
```

```python
import math
from contextlib import ExitStack

import concourse.bass as bass
from concourse import mybir

ALU = mybir.AluOpType
ACT = mybir.ActivationFunctionType
F32 = mybir.dt.float32
I32 = mybir.dt.int32
U32 = mybir.dt.uint32
AX_X = mybir.AxisListType.X

P = 128
T = 256
TT = T // P
D = 1024
KD = D // P
DEPTH = 2
EPS = 1e-6
NEG = -1e30

SLOTS = 8
U_PARAMS, N_PARAMS = 0, 2
U_ADA, N_ADA = 2, 48
U_IN, N_IN = 50, 14
U_OUT, N_OUT = 64, 8
U_WQ, N_WQ = 72, 16
U_EXP, N_EXP = 88, 256
PER_LAYER = U_EXP + N_EXP
BASE2 = DEPTH * PER_LAYER
V_IN, N_IN2 = 0, 22
V_OUT = 22
V_XQ, V_XK, V_XV, V_XO = 30, 38, 46, 54
V_FFN, N_FF = 62, 22
UNITS2 = V_FFN + 3 * N_FF
UNITS = BASE2 + UNITS2
PAIRS = 64

L_N1, L_N2, L_BADA, L_QG, L_KG, L_CONV, L_PSC, L_SINK = 0, 8, 16, 64, 65, 66, 72, 74
L_COLS = 90
_at = 0


def _cols(n):
    global _at
    _at += n
    return _at - n


W_MIX, W_XA, W_MEM, W_FFN, W_FIN = (_cols(8) for _ in range(5))
W_CW, W_CB, W_SN, W_SD, W_UD = _cols(56), _cols(14), _cols(6), _cols(6), _cols(2)
W_FW, W_FB = _cols(66), _cols(22)
W_LR, W_LI, W_DT = _cols(8), _cols(8), _cols(8)
W_DTB, W_ALOG = _cols(12), _cols(12)
W_COLS = _at
_at = 0
C_ID, C_ONE, C_BLK, C_ROT, C_TRI, C_CAUS = (_cols(128) for _ in range(6))
C_MASK, C_CNT, C_IOTA, C_I16, C_INV = _cols(512), _cols(512), _cols(128), _cols(16), _cols(1)
C_COLS = _at


class Steps:

    def __init__(self, eng, sems):
        self.eng, self.sems, self.n = eng, sems, {}

    def mark(self, ins, name):
        self.n[name] = self.n.get(name, 0) + 1
        ins.then_inc(self.sems(name), 1)

    def __call__(self, ins, name):
        self.mark(ins, name)
        self.wait(name, self.n[name])

    def wait(self, name, value):
        self.eng.wait_ge(self.sems(name), value)


def program(nc, wstream, consts, xT, memT, cT, pos, vec2, s5b, s5c, wglu, wdt, out):
    ctx = ExitStack()
    with ctx:
        def sb(name, shape, dt=F32):
            return ctx.enter_context(nc.sbuf_tensor(name, shape, dt))

        X = sb("residual", [P, KD, T])
        H = sb("normed", [P, KD, T])
        RING = sb("ring", [P, SLOTS, D])
        AR = sb("arena", [P, P * T])
        WK = sb("work", [P, 2, 1024])
        CST = sb("consts_sb", [P, C_COLS])
        LV = sb("layer_vectors", [P, L_COLS])
        PK = sb("pool_and_keys", [P, 512])
        MOD = sb("modulation", [P, 48])
        S1G = sb("scale_gain", [P, 16])
        CA = sb("c_act", [P, 2, KD])
        RS = sb("rstd", [P, 3, T])
        COSSIN = sb("rope", [P, 2, T])
        J = sb("routes", [P, 3, T])
        PS = ctx.enter_context(nc.psum_tensor("banks", [P, 8, 512], F32))

        loaded = [ctx.enter_context(nc.semaphore(f"loaded{i}")) for i in range(SLOTS)]
        units_used = ctx.enter_context(nc.semaphore("units_used"))
        pool_of = [ctx.enter_context(nc.semaphore(f"stage{i}")) for i in range(120)]
        named = {}

        def S(name):
            if name not in named:
                named[name] = pool_of[len(named)]
            return named[name]

        def end_of_block():
            nums = sorted(s.num for s in pool_of)
            assert nums[-1] - nums[0] == len(nums) - 1
            nc.gpsimd.sem_clear(range(nums[0], nums[-1] + 1))
            nc.all_engine_barrier()
            named.clear()

        def col(t, c):
            return t[:, c:c + 1]

        ident = CST[:, C_ID:C_ID + P]
        ones = CST[:, C_ONE:C_ONE + P]
        blk64 = CST[:, C_BLK:C_BLK + P]
        rot = CST[:, C_ROT:C_ROT + P]
        tri = CST[:, C_TRI:C_TRI + P]
        causal = CST[:, C_CAUS:C_CAUS + P]
        mask = CST[:, C_MASK:C_MASK + 512]
        inv_cnt = CST[:, C_CNT:C_CNT + 512].rearrange("p (a t) -> p a t", a=2)
        iota = CST[:, C_IOTA:C_IOTA + P]
        iota16 = CST[:, C_I16:C_I16 + 16]
        invf = CST[:, C_INV:C_INV + 1]

        class Arena:
            def __init__(self):
                self.at = 0

            def __call__(self, *shape, dt=F32):
                n = int(math.prod(shape))
                o, self.at = self.at, self.at + n
                assert self.at <= P * T
                v = AR[:, o:o + n]
                if dt != F32:
                    v = v.bitcast(dt)
                names = "abcd"[:len(shape)]
                if len(shape) == 1:
                    return v
                return v.rearrange(f"p ({' '.join(names)}) -> p {' '.join(names)}",
                                   **{k: s for k, s in zip(names[1:], shape[1:])})

        def stream(sp, base, u0, u1):
            def one(u, s):
                sp.wait_ge(units_used, u - (SLOTS - 1))
                sp.dma_start(RING[:, s, :], wstream[u]).then_inc(loaded[s], 16)
            n = (u1 - u0) // SLOTS
            if n > 1:
                with sp.Fori(0, n) as r:
                    for s in range(SLOTS):
                        one(r * SLOTS + (base + u0 + s), (u0 + s) % SLOTS)
                u0 += n * SLOTS
            for u in range(u0, u1):
                one(base + u, u % SLOTS)

        def arrived(eng, base, u):
            eng.wait_ge(loaded[u % SLOTS], base * (16 // SLOTS) + 16 * (u // SLOTS + 1))

        def used(base, u):
            return base + (u + 1)

        class Tiles:

            def __init__(self):
                self.n = 0

            def bank(self, pe):
                if self.n >= 4:
                    pe.wait_ge(S("bank_emptied"), self.n - 3)
                self.n += 1
                return 2 + (self.n - 1) % 4

            def linear(self, pe, base, u0, n, rhs):
                for i in range(n):
                    b = self.bank(pe)
                    arrived(pe, base, u0 + i)
                    for k in range(KD):
                        mm = pe.matmul(PS[:, b, 0:T], RING[:, (u0 + i) % SLOTS, k * P:(k + 1) * P],
                                       rhs[:, k, :], start=(k == 0), stop=(k == KD - 1))
                    mm.then_inc(units_used, 1)

        class Drain:

            def __init__(self, eng):
                self.eng, self.n = eng, 0

            def __call__(self):
                self.n += 1
                return 2 + (self.n - 1) % 4

        def norm_squares(act, src, sq, name):
            act(nc.scalar.activation(sq, src, ACT.Square), name + "_squares")

        def norm_sum(pe, sq, n, name, bank=1):
            pe.wait_ge(S(name + "_squares"), 1)
            for k in range(n):
                mm = pe.matmul(PS[:, bank, 0:T], ones, sq[:, k, :], start=(k == 0), stop=(k == n - 1))
            mm.then_inc(S(name + "_sum"), 1)

        def norm_inverse(v, width, name, bank=1):
            v.wait(name + "_sum", 1)
            v(nc.vector.tensor_scalar(RS[:, 0, :], PS[:, bank, 0:T], 1.0 / width, EPS, ALU.mult, ALU.add),
              name + "_var")
            v(nc.vector.reciprocal(RS[:, 1, :], RS[:, 0, :]), name + "_inverse")

        def norm_root(act, name):
            act.wait(name + "_inverse", 1)
            act(nc.scalar.activation(RS[:, 2, :], RS[:, 1, :], ACT.Sqrt), name + "_rstd")

        def norm_apply(v, dst, src, gain, shift, name):
            v.wait(name + "_rstd", 1)
            v(nc.vector.tensor_tensor(dst, src, RS[:, 2:3, :].to_broadcast([P, KD, T]), ALU.mult),
              name + "_scaled")
            for k in range(KD):
                if shift is None:
                    i = nc.vector.tensor_scalar(dst[:, k, :], dst[:, k, :], col(gain, k), None, ALU.mult)
                else:
                    i = nc.vector.tensor_scalar(dst[:, k, :], dst[:, k, :], col(gain, k), col(shift, k),
                                                ALU.mult, ALU.add)
                v.mark(i, name + "_applied")
            v.wait(name + "_applied", KD)

        def reduce_angle(v, r, a, t):
            v(nc.vector.tensor_scalar(t, a, 1.0 / (2 * math.pi), 12582912.0, ALU.mult, ALU.add), "angle")
            v(nc.vector.tensor_scalar(t, t, -12582912.0, None, ALU.add), "angle")
            src = a
            for c in (6.28125, 0.00193405151367187500, 2 * math.pi - 6.28125 - 0.00193405151367187500):
                v(nc.vector.scalar_tensor_tensor(r, t, -c, src, ALU.mult, ALU.add), "angle")
                src = r
            v(nc.vector.tensor_scalar(r, r, -3.1415925, 3.1415925, ALU.max, ALU.min), "angle")

        def quarter_turn(v, r2, r, t):
            v(nc.vector.tensor_scalar(r2, r, math.pi / 2, None, ALU.add), "angle")
            v(nc.vector.tensor_scalar(t, r2, math.pi, -2 * math.pi, ALU.is_gt, ALU.mult), "angle")
            v(nc.vector.tensor_tensor(r2, r2, t, ALU.add), "angle")
            v(nc.vector.tensor_scalar(r2, r2, -3.1415925, 3.1415925, ALU.max, ALU.min), "angle")

        a0 = Arena()
        posi, posf, ang, tmp, red, red2 = a0(T, dt=I32), a0(T), a0(T), a0(T), a0(T), a0(T)
        with nc.Block() as block:
            @block.sync
            def _(sp):
                sp.dma_start(CST[:, :], consts).then_inc(S("inputs"), 16)
                sp.dma_start(X[:, :, :], xT).then_inc(S("inputs"), 16)
                sp.dma_start(CA[:, 0, :], cT).then_inc(S("inputs"), 16)
                sp.dma_start(posi, pos).then_inc(S("inputs"), 16)
                for u in range(SLOTS):
                    sp.dma_start(RING[:, u, :], wstream[u]).then_inc(loaded[u], 16)

            @block.vector
            def _(dve):
                v = Steps(dve, S)
                v.wait("inputs", 64)
                v(dve.tensor_copy(posf, posi), "pos")
                v(dve.tensor_scalar(ang, posf, invf, None, ALU.mult), "pos")
                reduce_angle(v, red, ang, tmp)
                quarter_turn(v, red2, red, tmp)

            @block.scalar
            def _(sc):
                act = Steps(sc, S)
                act.wait("inputs", 64)
                act(sc.activation(CA[:, 1, :], CA[:, 0, :], ACT.Silu), "c_act")
                act.wait("angle", 10)
                act(sc.activation(COSSIN[:, 0, :], red2, ACT.Sin), "tables")
                act(sc.activation(COSSIN[:, 1, :], red, ACT.Sin), "tables")
        end_of_block()

        with nc.Fori(0, DEPTH) as layer:
            base = layer * PER_LAYER

            a = Arena()
            Z = a(14, T)
            SQ = a(KD, T)
            QSQ, QVAR, QN, QR, QT = (a(5, T) for _ in range(5))
            SC = a(16, T)
            MX, NMX, ESK, SUM = a(16), a(16), a(16), a(16)
            PT = a(8, 2, T)
            VP = a(2, 2, P)
            CU = a(2, T + 2)
            CY = a(2, T)
            PU, P2, P4, P8, P16 = (a(2, T + 16) for _ in range(5))
            PL = a(2, T)
            MIX = a(8, T)
            with nc.Block() as block:
                @block.sync
                def _(sp):
                    stream(sp, base, SLOTS, U_WQ + SLOTS)

                @block.gpsimd
                def _(pool):
                    pool.memset(VP, 0.0).then_inc(S("cleared"), 1)
                    pool.memset(CU, 0.0).then_inc(S("cleared"), 1)
                    pool.memset(PU, 0.0).then_inc(S("cleared"), 1)

                @block.tensor
                def _(pe):
                    pe.wait_ge(units_used, base + N_PARAMS)
                    norm_sum(pe, SQ, KD, "n1")
                    with pe.Fori(0, N_ADA // SLOTS) as r:
                        for s in range(SLOTS):
                            u = U_ADA + s
                            pe.wait_ge(loaded[u % SLOTS], base * (16 // SLOTS) + 16 * (u // SLOTS + 1) + 16 * r)
                            for k in range(KD):
                                mm = pe.matmul(PS[:, 0, bass.ds(r * SLOTS + s, 1)],
                                               RING[:, u % SLOTS, k * P:(k + 1) * P], CA[:, 1, k:k + 1],
                                               start=(k == 0), stop=(k == KD - 1))
                            mm.then_inc(units_used, 1)
                    pe.wait_ge(S("n1_applied"), KD)
                    tiles = Tiles()
                    tiles.linear(pe, base, U_IN, N_IN, H)
                    pe.wait_ge(S("qk_squares"), 1)
                    for i in range(5):
                        b = tiles.bank(pe)
                        pe.matmul(PS[:, b, 0:T], blk64, QSQ[:, i, :], start=True, stop=True)\
                            .then_inc(S("qk_sums"), 1)
                    pe.wait_ge(S("qk_normed"), 2)
                    for i in range(5):
                        b = tiles.bank(pe)
                        pe.matmul(PS[:, b, 0:T], rot, QN[:, i, :], start=True, stop=True)\
                            .then_inc(S("qk_rotated"), 1)
                    b = tiles.bank(pe)
                    for kt in range(TT):
                        mm = pe.transpose(PS[:, b, kt * P:(kt + 1) * P], Z[:, 5, kt * P:(kt + 1) * P], ident)
                    mm.then_inc(S("v_turned"), 1)
                    pe.wait_ge(S("qk_roped"), 1)
                    for hh in range(8):
                        j, half = hh // 2, hh % 2
                        rows = slice(64 * half, 64 * half + 64)
                        b = tiles.bank(pe)
                        for qt in range(TT):
                            mm = pe.matmul(PS[:, b, qt * T:(qt + 1) * T], QR[rows, j, qt * P:(qt + 1) * P],
                                           QR[rows, 4, :], start=True, stop=True)
                        mm.then_inc(S("scored"), 1)
                    pe.wait_ge(S("pooled"), 1)
                    for i in range(2):
                        b = tiles.bank(pe)
                        pe.matmul(PS[:, b, 0:T], PK[:, i * P:(i + 1) * P], PL[:, i, :], start=True, stop=True)\
                            .then_inc(S("pool_mixed"), 1)
                    pe.wait_ge(S("probs"), 1)
                    for hh in range(8):
                        b = tiles.bank(pe)
                        for kt in range(TT):
                            for qt in range(TT):
                                mm = pe.transpose(PS[:, b, kt * T + qt * P:kt * T + (qt + 1) * P],
                                                  SC[:, 2 * hh + qt, kt * P:(kt + 1) * P], ident)
                        mm.then_inc(S("probs_turned"), 1)
                    pe.wait_ge(S("v_padded"), 1)
                    pe.wait_ge(S("bank_emptied"), tiles.n)
                    for j in range(4):
                        b = tiles.bank(pe)
                        for n in range(4):
                            half, kt = n // 2, n % 2
                            mm = pe.matmul(PS[:, b, 0:T], VP[:, kt, half, :], PT[:, 2 * j + half, kt, :],
                                           start=(n == 0), stop=(n == 3))
                        mm.then_inc(S("attended"), 1)
                    pe.wait_ge(S("conv_mixed"), 2)
                    pe.wait_ge(S("bank_emptied"), tiles.n)
                    tiles.linear(pe, base, U_OUT, N_OUT, MIX)

                @block.scalar
                def _(sc):
                    act = Steps(sc, S)
                    arrived(sc, base, 0)
                    sc.activation(LV[:, :], RING[:, 0, 0:L_COLS], ACT.Copy).then_inc(units_used, 1)
                    arrived(sc, base, 1)
                    sc.activation(PK[:, :], RING[:, 1, 0:512], ACT.Copy).then_inc(units_used, 1)
                    norm_squares(act, X[:, :, :], SQ, "n1")
                    norm_root(act, "n1")
                    nxt = Drain(sc)
                    for i in range(N_IN):
                        sc.wait_ge(units_used, used(base, U_IN + i))
                        b = nxt()
                        act.mark(sc.activation(Z[:, i, :], PS[:, b, 0:T], ACT.Copy), "bank_emptied")
                    act.wait("bank_emptied", N_IN)
                    act(sc.activation(QSQ, Z[:, 0:5, :], ACT.Square), "qk_squares")
                    act.wait("qk_inverse", 1)
                    act(sc.activation(QVAR, QVAR, ACT.Sqrt), "qk_rstd")
                    act.wait("maxes", 2)
                    act(sc.activation(ESK, ESK, ACT.Exp), "sink_exp")
                    for i in range(16):
                        act.mark(sc.activation(SC[:, i, :], SC[:, i, :], ACT.Exp, bias=NMX[:, i:i + 1],
                                               accum_out=SUM[:, i:i + 1]), "exps")

                @block.vector
                def _(dve):
                    v = Steps(dve, S)
                    dve.wait_ge(units_used, base + N_PARAMS)
                    norm_inverse(v, D, "n1")
                    dve.wait_ge(units_used, used(base, U_ADA + N_ADA - 1))
                    v(dve.tensor_tensor(MOD[:, :], PS[:, 0, 0:48], LV[:, L_BADA:L_BADA + 48], ALU.add), "mod")
                    v(dve.tensor_scalar(S1G[:, 0:8], MOD[:, 8:16], 1.0, None, ALU.add), "mod")
                    v(dve.tensor_scalar(S1G[:, 8:16], MOD[:, 32:40], 1.0, None, ALU.add), "mod")
                    v(dve.tensor_tensor(S1G[:, 0:8], S1G[:, 0:8], LV[:, L_N1:L_N1 + 8], ALU.mult), "mod")
                    v(dve.tensor_tensor(S1G[:, 8:16], S1G[:, 8:16], LV[:, L_N2:L_N2 + 8], ALU.mult), "mod")
                    norm_apply(v, H[:, :, :], X[:, :, :], S1G[:, 0:8], MOD[:, 0:8], "n1")
                    nxt = Drain(dve)
                    nxt.n = N_IN
                    v.n["bank_emptied"] = N_IN
                    for i in range(5):
                        v.wait("qk_sums", i + 1)
                        v(dve.tensor_scalar(QVAR[:, i, :], PS[:, nxt(), 0:T], 1.0 / 64, EPS, ALU.mult, ALU.add),
                          "bank_emptied")
                    v(dve.reciprocal(QVAR, QVAR), "qk_inverse")
                    v.wait("qk_rstd", 1)
                    v(dve.scalar_tensor_tensor(QN[:, 0:4, :], Z[:, 0:4, :], LV[:, L_QG:L_QG + 1], QVAR[:, 0:4, :],
                                               ALU.mult, ALU.mult), "qk_normed")
                    v(dve.scalar_tensor_tensor(QN[:, 4, :], Z[:, 4, :], LV[:, L_KG:L_KG + 1], QVAR[:, 4, :],
                                               ALU.mult, ALU.mult), "qk_normed")
                    v(dve.tensor_tensor(QR, QN, COSSIN[:, 0:1, :].to_broadcast([P, 5, T]), ALU.mult), "qk_cos")
                    for i in range(5):
                        v.wait("qk_rotated", i + 1)
                        v(dve.tensor_tensor(QT[:, i, :], PS[:, nxt(), 0:T], COSSIN[:, 1, :], ALU.mult),
                          "bank_emptied")
                    v(dve.tensor_tensor(QR, QR, QT, ALU.add), "qk_roped")
                    v.wait("v_turned", 1)
                    v.wait("cleared", 3)
                    b = nxt()
                    vt = PS[:, b, 0:T].rearrange("p (k h d) -> p k h d", k=2, h=2)
                    v(dve.tensor_copy(VP[:, :, 0, 0:64], vt[:, :, 0, :]), "v_padded")
                    v(dve.tensor_copy(VP[:, :, 1, 64:128], vt[:, :, 1, :]), "bank_emptied")
                    for hh in range(8):
                        v.wait("scored", hh + 1)
                        v(dve.scalar_tensor_tensor(SC[:, 2 * hh:2 * hh + 2, :].rearrange("p a b -> p (a b)"),
                                                   PS[:, nxt(), :], 0.125, mask, ALU.mult, ALU.add), "bank_emptied")
                    v(dve.tensor_reduce(MX, SC, AX_X, ALU.max), "max")
                    v(dve.tensor_tensor(MX, MX, LV[:, L_SINK:L_SINK + 16], ALU.max), "max")
                    v(dve.tensor_scalar(NMX, MX, -1.0, None, ALU.mult), "maxes")
                    v(dve.tensor_tensor(ESK, LV[:, L_SINK:L_SINK + 16], MX, ALU.subtract), "maxes")
                    v(dve.tensor_tensor(CU[:, :, 1:T + 1], Z[:, 10:12, :], Z[:, 6:8, :], ALU.mult), "conv")
                    for i in range(2):
                        w = [LV[:, L_CONV + 2 * n + i:L_CONV + 2 * n + i + 1] for n in range(3)]
                        v(dve.tensor_scalar(CY[:, i, :], CU[:, i, 0:T], w[0], None, ALU.mult), "conv")
                        for n in (1, 2):
                            v(dve.scalar_tensor_tensor(CY[:, i, :], CU[:, i, n:n + T], w[n], CY[:, i, :],
                                                       ALU.mult, ALU.add), "conv")
                        v(dve.tensor_tensor(MIX[:, 4 + i, :], CY[:, i, :], Z[:, 8 + i, :], ALU.mult), "conv_mixed")
                    v(dve.tensor_copy(PU[:, :, 8:8 + T], Z[:, 12:14, :]), "pool")
                    for dst, src, lo, m, n in ((P2, PU, 1, 1, 0), (P4, P2, 2, 1, 1), (P8, P4, 4, 2, 2),
                                               (P16, P8, 8, 4, 4)):
                        hi = T + 16 - lo
                        v(dve.tensor_tensor(dst[:, :, lo:hi], src[:, :, lo - m:hi - m], src[:, :, lo + n:hi + n],
                                            ALU.add), "pool")
                    for g, src in enumerate((P2, P4, P8, P16)):
                        r = slice(64 * (g % 2), 64 * (g % 2) + 64)
                        v(dve.tensor_tensor(PL[r, g // 2, :], src[r, g // 2, 8:8 + T], inv_cnt[r, g // 2, :],
                                            ALU.mult), "pool")
                    v(dve.tensor_tensor(PL, PL, Z[:, 12:14, :], ALU.subtract), "pooled")
                    for i in range(2):
                        v.wait("pool_mixed", i + 1)
                        v(dve.tensor_scalar(MIX[:, 6 + i, :], PS[:, nxt(), 0:T], LV[:, L_PSC + i:L_PSC + i + 1],
                                            None, ALU.mult), "bank_emptied")
                    v.wait("exps", 16)
                    v.wait("sink_exp", 1)
                    v(dve.tensor_tensor(SUM, SUM, ESK, ALU.add), "soft")
                    v(dve.reciprocal(SUM, SUM), "soft")
                    v(dve.tensor_tensor(SC, SC, SUM.unsqueeze(2).to_broadcast([P, 16, T]), ALU.mult), "probs")
                    for hh in range(8):
                        v.wait("probs_turned", hh + 1)
                        v(dve.tensor_copy(PT[:, hh, :, :].rearrange("p a b -> p (a b)"), PS[:, nxt(), :]),
                          "bank_emptied")
                    for j in range(4):
                        v.wait("attended", j + 1)
                        v(dve.tensor_copy(MIX[:, j, :], PS[:, nxt(), 0:T]), "bank_emptied")
                    for i in range(N_OUT):
                        dve.wait_ge(units_used, used(base, U_OUT + i))
                        v.mark(dve.scalar_tensor_tensor(X[:, i, :], PS[:, nxt(), 0:T], col(MOD[:, 16:24], i),
                                                        X[:, i, :], ALU.mult, ALU.add), "bank_emptied")
                    v.wait("bank_emptied", nxt.n)
            end_of_block()

            a = Arena()
            SQ = a(KD, T)
            Q = a(16, T)
            KS = a(32, P)
            V16 = a(32, 16)
            I16 = a(32, 16, dt=U32)
            I16F = a(32, 16)
            CAND = a(16, 16, 16)
            TOP = a(16, 16)
            POS, PA, PB = a(16, 16, dt=U32), a(16, 16, dt=U32), a(16, 16, dt=U32)
            AF, BF = a(T), a(T)
            OH = a(T, 16)
            SEL = a(2, T)
            GT = a(16, 16)
            GS = a(16)
            with nc.Block() as block:
                @block.sync
                def _(sp):
                    stream(sp, base, U_WQ + SLOTS, U_EXP + SLOTS)

                @block.tensor
                def _(pe):
                    norm_sum(pe, SQ, KD, "n2")
                    pe.wait_ge(S("n2_applied"), KD)
                    tiles = Tiles()
                    tiles.linear(pe, base, U_WQ, N_WQ, H)
                    pe.wait_ge(S("bank_emptied"), N_WQ)
                    for n in range(8):
                        b = tiles.bank(pe)
                        for m in range(4):
                            tt, hh = (4 * n + m) // 16, (4 * n + m) % 16
                            mm = pe.matmul(PS[:, b, m * P:(m + 1) * P], Q[:, hh, tt * P:(tt + 1) * P],
                                           PK[:, T + (hh % 2) * P:T + (hh % 2 + 1) * P], start=True, stop=True)
                        mm.then_inc(S("key_scored"), 1)
                    pe.wait_ge(S("routed"), 3)
                    for i, src in enumerate((SEL[:, 0, :], SEL[:, 1, :], GT.rearrange("p a b -> p (a b)"))):
                        b = tiles.bank(pe)
                        for tt in range(TT):
                            mm = pe.transpose(PS[:, b, tt * P:(tt + 1) * P], src[:, tt * P:(tt + 1) * P], ident)
                        mm.then_inc(S("routes_turned"), 1)

                @block.scalar
                def _(sc):
                    act = Steps(sc, S)
                    norm_squares(act, X[:, :, :], SQ, "n2")
                    norm_root(act, "n2")
                    nxt = Drain(sc)
                    for i in range(N_WQ):
                        sc.wait_ge(units_used, used(base, U_WQ + i))
                        act.mark(sc.activation(Q[:, i, :], PS[:, nxt(), 0:T], ACT.Copy), "bank_emptied")
                    for n in range(8):
                        act.wait("key_scored", n + 1)
                        act.mark(sc.activation(KS[:, 4 * n:4 * n + 4, :].rearrange("p a b -> p (a b)"),
                                               PS[:, nxt(), :], ACT.Copy), "bank_emptied")
                    act.wait("centred", 1)
                    act(sc.activation(GT, GT, ACT.Exp), "gate_exp")
                    for i in range(3):
                        act.wait("routes_turned", i + 1)
                        act.mark(sc.activation(J[:, i, :], PS[:, nxt(), 0:T], ACT.Copy), "bank_emptied")
                    act.wait("bank_emptied", nxt.n)

                @block.vector
                def _(dve):
                    v = Steps(dve, S)
                    norm_inverse(v, D, "n2")
                    norm_apply(v, H[:, :, :], X[:, :, :], S1G[:, 8:16], MOD[:, 24:32], "n2")

                    def top16(rows, src, val, idx):
                        for half in range(2):
                            o = slice(8 * half, 8 * half + 8)
                            for r in range(rows):
                                v.mark(dve.max(val[:, r, o], src(r)), "top")
                            v.wait("top", v.n["top"])
                            for r in range(rows):
                                v.mark(dve.max_index(idx[:, r, o], val[:, r, o], src(r)), "top")
                            if half == 0:
                                for r in range(rows):
                                    v.mark(dve.match_replace(src(r), val[:, r, o], src(r), -3e38), "top")
                            v.wait("top", v.n["top"])

                    v.wait("bank_emptied", N_WQ + 8)
                    top16(32, lambda r: KS[:, r, :], V16, I16)
                    v(dve.tensor_copy(I16F, I16), "pick")
                    pair = V16.rearrange("p (g h) k -> p g h k", h=2)
                    v(dve.tensor_tensor(CAND, pair[:, :, 0, :].unsqueeze(3).to_broadcast([P, 16, 16, 16]),
                                        pair[:, :, 1, :].unsqueeze(2).to_broadcast([P, 16, 16, 16]), ALU.add), "pick")
                    flat = CAND.rearrange("p g i j -> p g (i j)")
                    top16(16, lambda r: flat[:, r, :], TOP, POS)
                    v(dve.tensor_tensor(GT, TOP, TOP[:, :, 0:1].to_broadcast([P, 16, 16]), ALU.subtract), "centred")
                    v(dve.tensor_scalar(PA, POS, 4, None, ALU.logical_shift_right), "pick")
                    v(dve.tensor_scalar(PB, POS, 15, None, ALU.bitwise_and), "pick")
                    ipair = I16F.rearrange("p (g h) k -> p g h k", h=2)
                    for n, (pi, pf) in enumerate(((PA, AF), (PB, BF))):
                        v(dve.tensor_copy(pf, pi.rearrange("p a b -> p (a b)")), "pick")
                        v(dve.tensor_tensor(OH, pf.unsqueeze(2).to_broadcast([P, T, 16]),
                                            iota16.unsqueeze(1).to_broadcast([P, T, 16]), ALU.is_equal), "pick")
                        oh4 = OH.rearrange("p (g k) j -> p g k j", g=16)
                        v(dve.tensor_tensor(oh4, oh4, ipair[:, :, n, :].unsqueeze(2).to_broadcast([P, 16, 16, 16]),
                                            ALU.mult), "pick")
                        v(dve.tensor_reduce(SEL[:, n, :], OH, AX_X, ALU.add), "routed")
                    v.wait("gate_exp", 1)
                    v(dve.tensor_reduce(GS, GT, AX_X, ALU.add), "gate")
                    v(dve.reciprocal(GS, GS), "gate")
                    v(dve.tensor_tensor(GT, GT, GS.unsqueeze(2).to_broadcast([P, 16, 16]), ALU.mult), "routed")
            end_of_block()

            G = AR[:, :].rearrange("p (i t) -> p i t", i=P)
            hot = WK[:, :, :].rearrange("p s (m t i) -> p s m t i", m=2, t=4)
            with nc.Block() as block:
                def group(eng_body):
                    for s in range(2):
                        eng_body(s, s, True)

                @block.vector
                def _(dve):
                    def body(g, s, first):
                        if not first:
                            dve.wait_ge(S("g_made"), g - 1)
                        for t in range(4):
                            dve.tensor_scalar(hot[:, s, 0, t, :], iota, J[:, 0, bass.ds(g * 4 + t, 1)], None,
                                              ALU.is_equal)
                            i = dve.tensor_scalar(hot[:, s, 1, t, :], iota, J[:, 1, bass.ds(g * 4 + t, 1)],
                                                  J[:, 2, bass.ds(g * 4 + t, 1)], ALU.is_equal, ALU.mult)
                        i.then_inc(S("one_hots"), 1)
                    group(body)
                    with dve.Fori(1, T // 8) as r:
                        for s in range(2):
                            body(r * 2 + s, s, False)

                @block.tensor
                def _(pe):
                    def body(g, s, first):
                        pe.wait_ge(S("one_hots"), g + 1)
                        if not first:
                            pe.wait_ge(S("g_copied"), g - 1)
                        for t in range(4):
                            mm = pe.matmul(PS[:, s, t * P:(t + 1) * P], hot[:, s, 0, t, :], hot[:, s, 1, t, :],
                                           start=True, stop=True)
                        mm.then_inc(S("g_made"), 1)
                    group(body)
                    with pe.Fori(1, T // 8) as r:
                        for s in range(2):
                            body(r * 2 + s, s, False)

                @block.scalar
                def _(sc):
                    def body(g, s, first):
                        sc.wait_ge(S("g_made"), g + 1)
                        sc.activation(G[:, :, bass.ds(g * 4, 4)],
                                      PS[:, s, :].rearrange("p (t i) -> p i t", t=4), ACT.Copy)\
                            .then_inc(S("g_copied"), 1)
                    group(body)
                    with sc.Fori(1, T // 8) as r:
                        for s in range(2):
                            body(r * 2 + s, s, False)
                    sc.wait_ge(S("g_copied"), T // 4)
            end_of_block()

            with nc.Block() as block:
                E = WK[:, :, 0:512]

                @block.sync
                def _(sp):
                    stream(sp, base, U_EXP + SLOTS, PER_LAYER + SLOTS)

                @block.tensor
                def _(pe):
                    def slot_wait(i, r):
                        pe.wait_ge(loaded[i % SLOTS], (base + U_EXP) * 2 + 16 * (i // SLOTS + 1) + 16 * r)

                    def first_product(i, r, bank):
                        for e in range(2):
                            slot_wait(i + e, r)
                            for k in range(KD):
                                mm = pe.matmul(PS[:, bank, e * T:(e + 1) * T],
                                               RING[:, (i + e) % SLOTS, k * P:(k + 1) * P], H[:, k, :],
                                               start=(k == 0), stop=(k == KD - 1))
                            mm.then_inc(units_used, 1)

                    def second_product(i, r, s, j, first=False, last=False):
                        pe.wait_ge(S("gated"), j + 1)
                        for e in range(2):
                            slot_wait(i + e, r)
                            for k in range(KD):
                                mm = pe.matmul(PS[:, 4 + k // 2, (k % 2) * T:(k % 2 + 1) * T],
                                               RING[:, (i + e) % SLOTS, k * P:(k + 1) * P],
                                               E[:, s, e * T:(e + 1) * T],
                                               start=(first and e == 0 and k % 2 == 0), stop=(last and e == 1),
                                               skip_group_check=True)
                            mm.then_inc(units_used, 1)

                    def step(r, q, peeled):
                        j = r * 2 + q
                        if not (peeled and q == 0):
                            pe.wait_ge(S("gelu_done"), j)
                        first_product(2 + 4 * q, r, 1 - q)
                        second_product(4 + 4 * q, r, q, j, first=peeled and q == 0)

                    first_product(0, 0, 0)
                    step(0, 0, True)
                    step(0, 1, True)
                    with pe.Fori(1, 31) as r:
                        step(r, 0, False)
                        step(r, 1, False)
                    step(31, 0, False)
                    second_product(6, 31, 1, 63, last=True)

                @block.scalar
                def _(sc):
                    def gelu(j, s, first, start=False):
                        sc.wait_ge(units_used, base + U_EXP + (2 if start else 4 * j))
                        sc.activation(E[:, s, :], PS[:, s, :], ACT.Gelu).then_inc(S("gelu_done"), 1)
                    gelu(0, 0, True, True)
                    gelu(1, 1, True)
                    with sc.Fori(1, PAIRS // 2) as r:
                        for s in range(2):
                            j = r * 2 + s
                            gelu(j, s, False)

                @block.vector
                def _(dve):
                    def gate(j, s):
                        dve.wait_ge(S("gelu_done"), j + 1)
                        dve.tensor_tensor(E[:, s, :], E[:, s, :],
                                          G[:, bass.ds(j * 2, 2), :].rearrange("p a b -> p (a b)"), ALU.mult)\
                            .then_inc(S("gated"), 1)
                    with dve.Fori(0, PAIRS // 2) as r:
                        for s in range(2):
                            gate(r * 2 + s, s)
                    dve.wait_ge(units_used, base + PER_LAYER)
                    for k in range(KD):
                        i = dve.scalar_tensor_tensor(X[:, k, :], PS[:, 4 + k // 2, (k % 2) * T:(k % 2 + 1) * T],
                                                     MOD[:, 40 + k:41 + k], X[:, k, :], ALU.mult, ALU.add)
                    i.then_inc(S("x_done"), 1)
                    dve.wait_ge(S("x_done"), 1)
            end_of_block()

        base = BASE2
        a = Arena()
        V2 = a(W_COLS)
        SB = a(2, 8, P)
        SCM = a(2, 8, P)
        GLU = a(2, T)
        WDT = a(KD, 12)
        keep = a.at
        ZU = a(8, T)
        here = a.at
        XP = a(14, T + 3)
        there, a.at = a.at, here
        SYQ, MIX = a(6, T), a(8, T)
        a.at = max(a.at, there)
        XC = a(14, T)
        S1, S2, S3, S4 = a(24), a(24), a(24), a(24)
        DTM, DA, ACS, LAST, NEGA = a(2, 12), a(2, 12), a(2, 12), a(2, 12), a(12)
        DEC = a(12)
        here = a.at
        SEG = a(2, 12, P)
        there, a.at = a.at, here
        SQ = a(KD, T)
        a.at = there
        ER1 = a(12, P)
        CB = a(4, 384)
        here = a.at
        M = a(12, 384)
        there, a.at = a.at, here
        HSC = a(8, 2, T)
        a.at = there
        XD = a(2, 12, P)
        C8 = [a(8) for _ in range(16)]
        PW = a(8, 2, 8)
        PWN = a(8, 8)
        B1, B2 = a(2, P + T), a(2, P + T)
        VT1 = a(T)
        UY = a(2, T)
        at = {}
        with nc.Block() as block:
            @block.sync
            def _(sp):
                stream(sp, base, SLOTS, V_XQ + SLOTS)

            @block.gpsimd
            def _(pool):
                for t in (XP, XD, B1, B2):
                    pool.memset(t, 0.0).then_inc(S("cleared"), 1)

            @block.tensor
            def _(pe):
                norm_sum(pe, SQ, KD, "m")
                pe.wait_ge(S("m_applied"), KD)
                tiles = Tiles()
                tiles.linear(pe, base, V_IN, N_IN2, H)
                b = tiles.bank(pe)
                pe.wait_ge(S("small"), 80)
                for tt in range(TT):
                    for k in range(KD):
                        mm = pe.matmul(PS[:, b, tt * 12:tt * 12 + 12], H[:, k, tt * P:(tt + 1) * P], WDT[:, k, :],
                                       start=(k == 0), stop=(k == KD - 1))
                mm.then_inc(S("dt_raw"), 1)
                pe.wait_ge(S("da"), 1)
                b = tiles.bank(pe)
                for c in range(TT):
                    pe.matmul(PS[:, b, c * 12:c * 12 + 12], tri, DA[:, c, :], start=True, stop=True)
                    mm = pe.matmul(PS[:, b, 24 + c * 12:36 + c * 12], ones, DA[:, c, :], start=True, stop=True)
                mm.then_inc(S("cumulated"), 1)
                for c in range(TT):
                    for n in range(3):
                        b = tiles.bank(pe)
                        for m in range(4):
                            h = 4 * n + m
                            mm = pe.matmul(PS[:, b, m * P:(m + 1) * P],
                                           DA[:, c, h:h + 1].to_broadcast([P, P]), tri, start=True, stop=True)
                        mm.then_inc(S("rows"), 1)
                pe.wait_ge(S("xbc"), 14)
                for g in range(4):
                    b = tiles.bank(pe)
                    pe.matmul(PS[:, b, 0:T], XC[:, 6 + g, 0:P], XC[:, 10 + g, :], start=True, stop=True)
                    pe.matmul(PS[:, b, T:384], XC[:, 6 + g, P:T], XC[:, 10 + g, P:T], start=True, stop=True)\
                        .then_inc(S("cb"), 1)
                for s in range(TT):
                    for n, m in ((0, 4), (4, 2)):
                        b = tiles.bank(pe)
                        for i in range(m):
                            mm = pe.transpose(PS[:, b, i * P:(i + 1) * P], XC[:, n + i, s * P:(s + 1) * P], ident)
                        mm.then_inc(S("x_turned"), 1)
                pe.wait_ge(S("bank_emptied"), tiles.n)
                pe.wait_ge(S("decayed"), 14)
                for i in range(6):
                    b = tiles.bank(pe)
                    for n, h in enumerate((2 * i, 2 * i + 1)):
                        pe.matmul(PS[:, b, 0:T], XD[:, 0, h, :], M[:, h, 0:T], start=(n == 0), stop=False,
                                  skip_group_check=True)
                        mm = pe.matmul(PS[:, b, P:T], XD[:, 1, h, :], M[:, h, T:384], start=False, stop=(n == 1),
                                       skip_group_check=True)
                    mm.then_inc(S("ssd_y"), 1)
                pe.wait_ge(S("ssd_squares"), 1)
                for k in range(6):
                    mm = pe.matmul(PS[:, 0, 0:T], ones, SYQ[:, k, :], start=(k == 0), stop=(k == 5))
                mm.then_inc(S("ssd_sum"), 1)
                for j in range(8):
                    b = tiles.bank(pe)
                    for n in range(2):
                        mm = pe.matmul(PS[:, b, n * T:(n + 1) * T], SB[:, n, j, :], ZU[:, j // 4, :],
                                       start=True, stop=True)
                    mm.then_inc(S("bu"), 1)
                pe.wait_ge(S("scanned"), 8)
                for f in range(2):
                    b = tiles.bank(pe)
                    for n in range(8):
                        j, part = 4 * f + n // 2, n % 2
                        mm = pe.matmul(PS[:, b, 0:T], SCM[:, part, j, :], HSC[:, j, part, :],
                                       start=(n == 0), stop=(n == 7))
                    mm.then_inc(S("s5_y"), 1)
                at["s5_y"] = tiles.n
                pe.wait_ge(S("s5_gelu"), 1)
                for f in range(2):
                    b = tiles.bank(pe)
                    for k in range(2):
                        mm = pe.matmul(PS[:, b, 0:T], GLU[:, k, f * P:(f + 1) * P], UY[:, k, :],
                                       start=(k == 0), stop=(k == 1))
                    mm.then_inc(S("glu"), 1)
                pe.wait_ge(S("mixed"), 8)
                tiles.linear(pe, base, V_OUT, 8, MIX)

            @block.scalar
            def _(sc):
                act = Steps(sc, S)
                for t, src in ((V2, vec2), (SB, s5b), (SCM, s5c), (GLU, wglu), (WDT, wdt)):
                    sc.dma_start(t, src).then_inc(S("small"), 16)
                act.wait("small", 80)
                norm_squares(act, X[:, :, :], SQ, "m")
                norm_root(act, "m")
                nxt = Drain(sc)
                act.wait("cleared", 4)
                for i in range(N_IN2):
                    sc.wait_ge(units_used, used(base, V_IN + i))
                    dst = ZU[:, i, :] if i < 8 else XP[:, i - 8, 3:3 + T]
                    act.mark(sc.activation(dst, PS[:, nxt(), 0:T], ACT.Copy), "bank_emptied")
                act.wait("dt_abs", 1)
                act(sc.activation(S3, S2, ACT.Exp, scale=-1.0), "dt_exp")
                act(sc.activation(NEGA, V2[:, W_ALOG:W_ALOG + 12], ACT.Exp), "a_exp")
                act(sc.activation(C8[0], V2[:, W_DT:W_DT + 8], ACT.Exp), "s5_dt")
                act.wait("dt_one", 1)
                act(sc.activation(S4, S4, ACT.Ln), "dt_ln")
                act.wait("decay_in", 1)
                act(sc.activation(DEC, DEC, ACT.Exp), "decay_exp")
                for n in range(6):
                    act.wait("rows", n + 1)
                    if n >= 3:
                        b = 2 + (N_IN2 + 2 + n) % 4
                        act(sc.activation(ER1[:, 4 * (n - 3):4 * (n - 2), :].rearrange("p a b -> p (a b)"),
                                          PS[:, b, :], ACT.Exp), "rows_exp")
                act.wait("bank_emptied", N_IN2 + 2 + 6)
                act.wait("segs", 18)
                act(sc.activation(SEG, SEG, ACT.Exp), "seg_exp")
                for i in range(14):
                    act.wait("convolved", i + 1)
                    act.mark(sc.activation(XC[:, i, :], XC[:, i, :], ACT.Silu,
                                           bias=V2[:, W_CB + i:W_CB + i + 1]), "xbc")
                act(sc.activation(ZU[:, 2:8, :], ZU[:, 2:8, :], ACT.Silu), "z_silu")
                act.wait("gated_y", 6)
                act(sc.activation(SYQ, MIX[:, 2:8, :], ACT.Square), "ssd_squares")
                act.wait("ssd_inverse", 1)
                act(sc.activation(RS[:, 2, :], RS[:, 1, :], ACT.Sqrt), "ssd_rstd")
                act.wait("angle", 10)
                act(sc.activation(C8[4], C8[4], ACT.Sin), "s5_cos")
                act(sc.activation(C8[3], C8[3], ACT.Sin), "s5_sin")
                act(sc.activation(C8[5], C8[5], ACT.Exp), "s5_mag")
                act.wait("bank_emptied", at["s5_y"])
                act(sc.activation(UY, UY, ACT.Gelu_apprx_tanh), "s5_gelu")
                for f in range(2):
                    act.wait("glu", f + 1)
                    act.mark(sc.activation(MIX[:, f, :], PS[:, 2 + (at["s5_y"] + f) % 4, 0:T], ACT.Sigmoid),
                             "bank_emptied")

            @block.vector
            def _(dve):
                v = Steps(dve, S)
                norm_inverse(v, D, "m")
                v.wait("small", 80)
                norm_apply(v, H[:, :, :], X[:, :, :], V2[:, W_MIX:W_MIX + 8], None, "m")
                nxt = Drain(dve)
                nxt.n = N_IN2
                v.wait("dt_raw", 1)
                v.n["bank_emptied"] = N_IN2
                v.wait("bank_emptied", N_IN2)
                raw = S1.rearrange("p (a b) -> p a b", a=2)
                v(dve.tensor_tensor(raw, PS[:, nxt(), 0:24].rearrange("p (a b) -> p a b", a=2),
                                    V2[:, W_DTB:W_DTB + 12].unsqueeze(1).to_broadcast([P, 2, 12]), ALU.add),
                  "bank_emptied")
                v(dve.tensor_scalar(S2, S1, -1.0, None, ALU.mult), "dt")
                v(dve.tensor_tensor(S2, S2, S1, ALU.max), "dt_abs")
                v.wait("dt_exp", 1)
                v(dve.tensor_scalar(S4, S3, 1.0, None, ALU.add), "dt")
                v(dve.tensor_scalar(S2, S4, -1.0, None, ALU.add), "dt_one")
                v.wait("dt_ln", 1)
                W1 = DTM.rearrange("p a b -> p (a b)")
                v(dve.tensor_scalar(W1, S2, 0.0, None, ALU.is_equal), "dt")
                v(dve.tensor_tensor(S2, S2, W1, ALU.add), "dt")
                v(dve.tensor_tensor(S4, S4, W1, ALU.add), "dt")
                v(dve.reciprocal(S2, S2), "dt")
                v(dve.tensor_tensor(S4, S4, S2, ALU.mult), "dt")
                v(dve.tensor_tensor(S4, S4, S3, ALU.mult), "dt")
                v(dve.scalar_tensor_tensor(W1, S1, 0.0, S4, ALU.max, ALU.add), "dt")
                v.wait("a_exp", 1)
                v(dve.tensor_scalar(NEGA, NEGA, -1.0, None, ALU.mult), "dt")
                v(dve.tensor_tensor(DA, DTM, NEGA.unsqueeze(1).to_broadcast([P, 2, 12]), ALU.mult), "da")
                v.wait("cumulated", 1)
                b = nxt()
                v(dve.tensor_copy(ACS, PS[:, b, 0:24].rearrange("p (a b) -> p a b", a=2)), "dt")
                v(dve.tensor_copy(LAST, PS[:, b, 24:48].rearrange("p (a b) -> p a b", a=2)), "bank_emptied")
                v(dve.tensor_tensor(DEC, LAST[:, 0, :], ACS[:, 0, :], ALU.subtract), "decay_in")
                LRr, LIi = C8[1], V2[:, W_LI:W_LI + 8]
                v(dve.tensor_scalar(LRr, V2[:, W_LR:W_LR + 8], -1e-4, None, ALU.min), "s5_lr")
                for n in range(6):
                    v.wait("rows", n + 1)
                    b = nxt()
                    c = n // 3
                    if c == 1:
                        v.wait("rows_exp", n - 2)
                    for m in range(4):
                        h = 4 * (n % 3) + m
                        v.mark(dve.scalar_tensor_tensor(SEG[:, c, h, :], PS[:, b, m * P:(m + 1) * P],
                                                        ACS[:, c, h:h + 1], causal, ALU.subtract, ALU.add),
                               "segs" if m < 3 else "bank_emptied")
                v.wait("bank_emptied", nxt.n)
                for i in range(14):
                    for n in range(4):
                        w = V2[:, W_CW + 14 * n + i:W_CW + 14 * n + i + 1]
                        if n == 0:
                            v(dve.tensor_scalar(XC[:, i, :], XP[:, i, 0:T], w, None, ALU.mult), "conv")
                        else:
                            v(dve.scalar_tensor_tensor(XC[:, i, :], XP[:, i, n:n + T], w, XC[:, i, :],
                                                       ALU.mult, ALU.add), "convolved" if n == 3 else "conv")
                for g in range(4):
                    v.wait("cb", g + 1)
                    v(dve.tensor_copy(CB[:, g, :], PS[:, nxt(), 0:384]), "bank_emptied")
                v.wait("seg_exp", 1)
                for g in range(4):
                    hs = slice(3 * g, 3 * g + 3)
                    for c, o in ((0, 0), (1, T)):
                        v.mark(dve.tensor_tensor(M[:, hs, o:o + P], SEG[:, c, hs, :],
                                                 CB[:, g:g + 1, o:o + P].to_broadcast([P, 3, P]), ALU.mult), "decayed")
                v.wait("decay_exp", 1)
                for h in range(12):
                    i = dve.scalar_tensor_tensor(M[:, h, P:T], CB[:, h // 3, P:T], DEC[:, h:h + 1], ER1[:, h, :],
                                                 ALU.mult, ALU.mult)
                    if h % 2:
                        v.mark(i, "decayed")
                for s in range(TT):
                    for n, m in ((0, 4), (4, 2)):
                        v.wait("x_turned", 2 * s + n // 4 + 1)
                        b = nxt()
                        src = PS[:, b, 0:m * P].rearrange("p (i h d) -> p i h d", i=m, h=2)
                        for q in range(2):
                            hsl = slice(2 * n + q, 2 * (n + m) + q - 1, 2)
                            i = dve.tensor_tensor(XD[:, s, hsl, 64 * q:64 * q + 64], src[:, :, q, :],
                                                  DTM[:, s, hsl].unsqueeze(2).to_broadcast([P, m, 64]), ALU.mult)
                            v.mark(i, "x_dt" if q == 0 else "bank_emptied")
                v.wait("z_silu", 1)
                for i in range(6):
                    v.wait("ssd_y", i + 1)
                    v(dve.scalar_tensor_tensor(MIX[:, 2 + i, :], XC[:, i, :], V2[:, W_SD + i:W_SD + i + 1],
                                               PS[:, nxt(), 0:T], ALU.mult, ALU.add), "bank_emptied")
                    v(dve.tensor_tensor(MIX[:, 2 + i, :], MIX[:, 2 + i, :], ZU[:, 2 + i, :], ALU.mult), "gated_y")
                norm_inverse(v, 6 * P, "ssd", bank=0)
                v.wait("ssd_rstd", 1)
                for i in range(6):
                    v(dve.scalar_tensor_tensor(MIX[:, 2 + i, :], MIX[:, 2 + i, :], V2[:, W_SN + i:W_SN + i + 1],
                                               RS[:, 2, :], ALU.mult, ALU.mult), "mixed")
                v.wait("s5_dt", 1)
                tt_ = lambda o, x, y, op: v(dve.tensor_tensor(o, x, y, op), "s5")
                th, red, red2, mag, t0 = C8[2], C8[3], C8[4], C8[5], C8[6]
                tt_(th, LIi, C8[0], ALU.mult)
                tt_(mag, LRr, C8[0], ALU.mult)
                reduce_angle(v, red, th, t0)
                quarter_turn(v, red2, red, t0)
                v.wait("s5_mag", 1)
                are, aim, den, am1, fre, fim = C8[8], C8[9], C8[10], C8[11], C8[12], C8[13]
                tt_(are, mag, red2, ALU.mult)
                tt_(aim, mag, red, ALU.mult)
                tt_(den, LRr, LRr, ALU.mult)
                tt_(t0, LIi, LIi, ALU.mult)
                tt_(den, den, t0, ALU.add)
                v(dve.tensor_scalar(am1, are, -1.0, None, ALU.add), "s5")
                tt_(fre, am1, LRr, ALU.mult)
                tt_(t0, aim, LIi, ALU.mult)
                tt_(fre, fre, t0, ALU.add)
                v(dve.reciprocal(den, den), "s5")
                tt_(fre, fre, den, ALU.mult)
                tt_(fim, aim, LRr, ALU.mult)
                tt_(t0, am1, LIi, ALU.mult)
                tt_(fim, fim, t0, ALU.subtract)
                tt_(fim, fim, den, ALU.mult)
                nfre, nfim = C8[14], C8[15]
                v(dve.tensor_scalar(nfre, fre, -1.0, None, ALU.mult), "s5")
                v(dve.tensor_scalar(nfim, fim, -1.0, None, ALU.mult), "s5")
                v(dve.tensor_copy(PW[:, 0, 0, :], are), "s5")
                v(dve.tensor_scalar(PW[:, 0, 1, :], aim, -1.0, None, ALU.mult), "s5")
                for k in range(7):
                    r0, i0 = PW[:, k, 0, :], PW[:, k, 1, :]
                    tt_(PW[:, k + 1, 0, :], r0, r0, ALU.mult)
                    tt_(t0, i0, i0, ALU.mult)
                    tt_(PW[:, k + 1, 0, :], PW[:, k + 1, 0, :], t0, ALU.subtract)
                    tt_(t0, r0, i0, ALU.mult)
                    v(dve.tensor_scalar(PW[:, k + 1, 1, :], t0, 2.0, None, ALU.mult), "s5")
                v(dve.tensor_scalar(PWN, PW[:, :, 1, :], -1.0, None, ALU.mult), "s5")
                for j in range(8):
                    sc1 = lambda t: t[:, j:j + 1]
                    v.wait("bu", j + 1)
                    b = nxt()
                    vre, vim = PS[:, b, 0:T], PS[:, b, T:2 * T]
                    v(dve.tensor_scalar(VT1, vim, sc1(fim), None, ALU.mult), "s5")
                    v(dve.scalar_tensor_tensor(B1[:, 0, P:], vre, sc1(fre), VT1, ALU.mult, ALU.subtract), "s5")
                    v(dve.tensor_scalar(VT1, vre, sc1(nfim), None, ALU.mult), "s5")
                    v(dve.scalar_tensor_tensor(B1[:, 1, P:], vim, sc1(nfre), VT1, ALU.mult, ALU.add), "bank_emptied")
                    src, dst = B1, B2
                    for k in range(8):
                        o = P - 2 ** k
                        final = k == 7
                        full = (lambda n: HSC[:, j, n, :]) if final else (lambda n: dst[:, n, P:])
                        both = HSC[:, j, :, :] if final else dst[:, :, P:]
                        pr, pi, pn = PW[:, k, 0, j:j + 1], PW[:, k, 1, j:j + 1], PWN[:, k, j:j + 1]
                        v(dve.scalar_tensor_tensor(both, src[:, :, o:o + T], pr, src[:, :, P:], ALU.mult, ALU.add), "s5")
                        v.mark(dve.scalar_tensor_tensor(full(0), src[:, 1, o:o + T], pn, full(0), ALU.mult, ALU.add), "s5")
                        v(dve.scalar_tensor_tensor(full(1), src[:, 0, o:o + T], pi, full(1), ALU.mult, ALU.add),
                          "scanned" if final else "s5")
                        src, dst = dst, src
                for f in range(2):
                    v.wait("s5_y", f + 1)
                    v(dve.scalar_tensor_tensor(UY[:, f, :], ZU[:, f, :], V2[:, W_UD + f:W_UD + f + 1],
                                               PS[:, nxt(), 0:T], ALU.mult, ALU.add), "bank_emptied")
                v.wait("bank_emptied", at["s5_y"] + 2)
                for f in range(2):
                    nxt()
                    v.mark(dve.tensor_tensor(MIX[:, f, :], MIX[:, f, :], UY[:, f, :], ALU.mult), "mixed")
                v.n["bank_emptied"] = nxt.n
                for i in range(8):
                    dve.wait_ge(units_used, used(base, V_OUT + i))
                    v.mark(dve.tensor_tensor(X[:, i, :], PS[:, nxt(), 0:T], X[:, i, :], ALU.add), "bank_emptied")
                v.wait("bank_emptied", nxt.n)
        end_of_block()

        a = Arena()
        a.at = keep
        MEM, MN, SQ, SQ2 = a(8, T), a(8, T), a(8, T), a(8, T)
        QX, KX, OX = a(8, T), a(8, T), a(8, T)
        VX = a(2, D)
        EX = a(8, T)
        MX, NMX, SUM = a(8), a(8), a(8)
        PTX = a(4, 2, T)
        with nc.Block() as block:
            @block.sync
            def _(sp):
                sp.dma_start(MEM, memT).then_inc(S("mem"), 16)
                stream(sp, base, V_XQ + SLOTS, V_FFN + SLOTS)

            @block.tensor
            def _(pe):
                norm_sum(pe, SQ, KD, "xa")
                pe.wait_ge(S("xa_applied"), KD)
                pe.wait_ge(S("xa_rstd"), 1)
                norm_sum(pe, SQ2, KD, "mem", bank=0)
                tiles = Tiles()
                tiles.linear(pe, base, V_XQ, 8, H)
                pe.wait_ge(S("mem_applied"), KD)
                tiles.linear(pe, base, V_XK, 8, MN)
                pe.wait_ge(S("bank_emptied"), 16)
                for k in range(KD):
                    arrived(pe, base, V_XV + k)
                    for mt in range(TT):
                        for n in range(2):
                            mm = pe.matmul(PS[:, 4 + 2 * mt + n, :], MN[:, k, mt * P:(mt + 1) * P],
                                           RING[:, (V_XV + k) % SLOTS, n * 512:(n + 1) * 512],
                                           start=(k == 0), stop=(k == KD - 1), skip_group_check=True)
                    mm.then_inc(units_used, 1)
                for h in range(4):
                    if h >= 2:
                        pe.wait_ge(S("exps"), 2 * (h - 1))
                    for qt in range(TT):
                        for k in range(2):
                            mm = pe.matmul(PS[:, h % 2, qt * T:(qt + 1) * T], QX[:, 2 * h + k, qt * P:(qt + 1) * P],
                                           KX[:, 2 * h + k, :], start=(k == 0), stop=(k == 1))
                    mm.then_inc(S("scored"), 1)
                pe.wait_ge(S("values"), 4)
                for h in range(4):
                    pe.wait_ge(S("probs"), h + 1)
                    b = tiles.bank(pe)
                    for mt in range(TT):
                        for qt in range(TT):
                            mm = pe.transpose(PS[:, b, mt * T + qt * P:mt * T + (qt + 1) * P],
                                              EX[:, 2 * h + qt, mt * P:(mt + 1) * P], ident)
                    mm.then_inc(S("probs_turned"), 1)
                for c in range(8):
                    b = tiles.bank(pe)
                    pe.wait_ge(S("bank_emptied"), 16 + c // 2 + 1)
                    for mt in range(TT):
                        mm = pe.matmul(PS[:, b, 0:T], VX[:, mt, c * P:(c + 1) * P], PTX[:, c // 2, mt, :],
                                       start=(mt == 0), stop=(mt == 1))
                    mm.then_inc(S("attended"), 1)
                pe.wait_ge(S("bank_emptied"), tiles.n)
                tiles.linear(pe, base, V_XO, 8, OX)

            @block.scalar
            def _(sc):
                act = Steps(sc, S)
                norm_squares(act, X[:, :, :], SQ, "xa")
                act.wait("mem", 16)
                norm_squares(act, MEM, SQ2, "mem")
                norm_root(act, "xa")
                norm_root(act, "mem")
                nxt = Drain(sc)
                for i in range(16):
                    sc.wait_ge(units_used, used(base, V_XQ + i))
                    dst = QX[:, i, :] if i < 8 else KX[:, i - 8, :]
                    act.mark(sc.activation(dst, PS[:, nxt(), 0:T], ACT.Copy), "bank_emptied")
                act.wait("bank_emptied", 16)
                sc.wait_ge(units_used, used(base, V_XV + 7))
                for n in range(4):
                    act.mark(sc.activation(VX[:, n // 2, (n % 2) * 512:(n % 2 + 1) * 512], PS[:, 4 + n, :], ACT.Copy),
                             "values")
                for h in range(4):
                    act.wait("maxed", h + 1)
                    for qt in range(TT):
                        i = 2 * h + qt
                        act.mark(sc.activation(EX[:, i, :], PS[:, h % 2, qt * T:(qt + 1) * T], ACT.Exp,
                                               bias=NMX[:, i:i + 1], scale=1.0 / 16, accum_out=SUM[:, i:i + 1]), "exps")

            @block.vector
            def _(dve):
                v = Steps(dve, S)
                norm_inverse(v, D, "xa")
                norm_apply(v, H[:, :, :], X[:, :, :], V2[:, W_XA:W_XA + 8], None, "xa")
                norm_inverse(v, D, "mem", bank=0)
                norm_apply(v, MN, MEM, V2[:, W_MEM:W_MEM + 8], None, "mem")
                for h in range(4):
                    v.wait("scored", h + 1)
                    v(dve.tensor_reduce(MX[:, 2 * h:2 * h + 2], PS[:, h % 2, :].rearrange("p (a b) -> p a b", a=2),
                                        AX_X, ALU.max), "max")
                    v(dve.tensor_scalar(NMX[:, 2 * h:2 * h + 2], MX[:, 2 * h:2 * h + 2], -1.0 / 16, None, ALU.mult),
                      "maxed")
                for h in range(4):
                    v.wait("exps", 2 * h + 2)
                    v(dve.reciprocal(SUM[:, 2 * h:2 * h + 2], SUM[:, 2 * h:2 * h + 2]), "inverse")
                    v(dve.tensor_tensor(EX[:, 2 * h:2 * h + 2, :], EX[:, 2 * h:2 * h + 2, :],
                                        SUM[:, 2 * h:2 * h + 2].unsqueeze(2).to_broadcast([P, 2, T]), ALU.mult), "probs")
                nxt = Drain(dve)
                nxt.n = 16
                v.n["bank_emptied"] = 16
                for h in range(4):
                    v.wait("probs_turned", h + 1)
                    v(dve.tensor_copy(PTX[:, h, :, :].rearrange("p a b -> p (a b)"), PS[:, nxt(), :]), "bank_emptied")
                for c in range(8):
                    v.wait("attended", c + 1)
                    v(dve.tensor_copy(OX[:, c, :], PS[:, nxt(), 0:T]), "bank_emptied")
                for i in range(8):
                    dve.wait_ge(units_used, used(base, V_XO + i))
                    v.mark(dve.tensor_tensor(X[:, i, :], PS[:, nxt(), 0:T], X[:, i, :], ALU.add), "bank_emptied")
                v.wait("bank_emptied", nxt.n)
        end_of_block()

        a = Arena()
        a.at = keep
        SQ = a(KD, T)
        GP = a(2, T + 2)
        CV = a(2, T)
        F = a(2, T)
        with nc.Block() as block:
            @block.sync
            def _(sp):
                stream(sp, base, V_FFN + SLOTS, UNITS2)
                sp.wait_ge(S("final_applied"), KD)
                sp.dma_start(out, H[:, :, :]).then_inc(S("stored"), 16)
                sp.wait_ge(S("stored"), 16)

            @block.gpsimd
            def _(pool):
                pool.memset(GP, 0.0).then_inc(S("cleared"), 1)

            @block.tensor
            def _(pe):
                norm_sum(pe, SQ, KD, "ff")
                pe.wait_ge(S("ff_applied"), KD)
                u = V_FFN

                def up(f, u):
                    if f >= 2:
                        pe.wait_ge(S("hidden"), f - 1)
                    for n in range(2):
                        arrived(pe, base, u + n)
                        for k in range(KD):
                            mm = pe.matmul(PS[:, 2 + f % 2, n * T:(n + 1) * T],
                                           RING[:, (u + n) % SLOTS, k * P:(k + 1) * P], H[:, k, :],
                                           start=(k == 0), stop=(k == KD - 1))
                        mm.then_inc(units_used, 1)
                    return u + 2

                def down(f, u):
                    pe.wait_ge(S("hidden"), f + 1)
                    arrived(pe, base, u)
                    for k in range(KD):
                        mm = pe.matmul(PS[:, 4 + k // 2, (k % 2) * T:(k % 2 + 1) * T],
                                       RING[:, u % SLOTS, k * P:(k + 1) * P], F[:, f % 2, :],
                                       start=(f == 0 and k % 2 == 0), stop=(f == N_FF - 1), skip_group_check=True)
                    mm.then_inc(units_used, 1)
                    return u + 1

                u = up(0, u)
                for f in range(1, N_FF):
                    u = up(f, u)
                    u = down(f - 1, u)
                u = down(N_FF - 1, u)
                assert u == UNITS2
                norm_sum(pe, SQ, KD, "final")

            @block.scalar
            def _(sc):
                act = Steps(sc, S)
                norm_squares(act, X[:, :, :], SQ, "ff")
                norm_root(act, "ff")
                act.wait("cleared", 1)
                for f in range(N_FF):
                    sc.wait_ge(units_used, used(base, V_FFN + (1 if f == 0 else 3 * f)))
                    if f >= 2:
                        act.wait("convolved", f - 1)
                    act.mark(sc.activation(GP[:, f % 2, 2:2 + T], PS[:, 2 + f % 2, 0:T], ACT.Copy), "g_copied")
                    act.wait("convolved", f + 1)
                    act(sc.activation(CV[:, f % 2, :], CV[:, f % 2, :], ACT.Silu,
                                      bias=V2[:, W_FB + f:W_FB + f + 1]), "silu")
                act.wait("x_done", KD)
                norm_squares(act, X[:, :, :], SQ, "final")
                norm_root(act, "final")

            @block.vector
            def _(dve):
                v = Steps(dve, S)
                norm_inverse(v, D, "ff")
                norm_apply(v, H[:, :, :], X[:, :, :], V2[:, W_FFN:W_FFN + 8], None, "ff")
                for f in range(N_FF):
                    s = f % 2
                    v.wait("g_copied", f + 1)
                    for n in range(3):
                        w = V2[:, W_FW + N_FF * n + f:W_FW + N_FF * n + f + 1]
                        if n == 0:
                            v(dve.tensor_scalar(CV[:, s, :], GP[:, s, 0:T], w, None, ALU.mult), "conv")
                        else:
                            v(dve.scalar_tensor_tensor(CV[:, s, :], GP[:, s, n:n + T], w, CV[:, s, :],
                                                       ALU.mult, ALU.add), "convolved" if n == 2 else "conv")
                    v.wait("silu", f + 1)
                    if f >= 2:
                        dve.wait_ge(units_used, used(base, V_FFN + 3 * (f - 2) + 4))
                    v(dve.tensor_tensor(F[:, s, :], CV[:, s, :], PS[:, 2 + s, T:2 * T], ALU.mult), "hidden")
                dve.wait_ge(units_used, used(base, UNITS2 - 1))
                for k in range(KD):
                    v.mark(dve.tensor_tensor(X[:, k, :], PS[:, 4 + k // 2, (k % 2) * T:(k % 2 + 1) * T],
                                             X[:, k, :], ALU.add), "x_done")
                norm_inverse(v, D, "final")
                norm_apply(v, H[:, :, :], X[:, :, :], V2[:, W_FIN:W_FIN + 8], None, "final")


def tables():
    import numpy as np

    c = np.zeros((P, C_COLS), np.float32)
    i = np.arange(P)
    c[:, C_ID:C_ID + P] = np.eye(P)
    c[:, C_ONE:C_ONE + P] = 1.0
    c[:, C_BLK:C_BLK + P] = i[:, None] // 64 == i[None] // 64
    r = np.zeros((P, P), np.float32)
    for h in (0, 64):
        for m in range(8):
            r[h + m + 8, h + m] = -1.0
            r[h + m, h + m + 8] = 1.0
    c[:, C_ROT:C_ROT + P] = r
    c[:, C_TRI:C_TRI + P] = i[:, None] <= i[None]
    c[:, C_CAUS:C_CAUS + P] = np.where(i[:, None] <= i[None], 0.0, NEG)
    t = np.arange(T)
    for qt in range(TT):
        far = np.abs((i + qt * P)[:, None] - t[None]) > 128
        c[:, C_MASK + qt * T:C_MASK + (qt + 1) * T] = np.where(far, NEG, 0.0)
    for g, w in enumerate((2, 4, 8, 16)):
        n = np.clip(t + w // 2, 0, T) - np.clip(t - w // 2, 0, T)
        c[64 * (g % 2):64 * (g % 2) + 64, C_CNT + (g // 2) * T:C_CNT + (g // 2 + 1) * T] = 1.0 / n
    c[:, C_IOTA:C_IOTA + P] = i
    c[:, C_I16:C_I16 + 16] = np.arange(16)
    inv = np.float32(500000.0) ** (-np.arange(0, 16, 2, dtype=np.float32) / np.float32(16))
    for h in (0, 8, 64, 72):
        c[h:h + 8, C_INV] = inv
    return c


def kernel(**inputs):
    import numpy as np
    import concourse.bacc as bacc
    from concourse.bass_utils import run_bass_kernel_spmd as run

    g = {k: np.asarray(v) for k, v in inputs.items()}

    def tiles(w):
        k, n = w.shape
        return w.reshape(k // P, P, n // P, P).transpose(2, 1, 0, 3).reshape(n // P, P, k)

    def by_part(x):
        return x.reshape(-1, P).T

    ws = np.zeros((UNITS, P, D), np.float32)
    heads = [j + 4 * half for j in range(4) for half in range(2)]
    perm = np.concatenate([np.arange(64) + 64 * h for h in heads])
    for l in range(DEPTH):
        b = l * PER_LAYER
        pv = ws[b]
        pv[:, L_N1:L_N1 + 8] = by_part(g["norm1_g"][l])
        pv[:, L_N2:L_N2 + 8] = by_part(g["norm2_g"][l])
        pv[:, L_BADA:L_BADA + 48] = by_part(g["b_ada"][l])
        pv[:, L_QG] = np.tile(g["q_norm_g"][l], 2)
        pv[:, L_KG] = np.tile(g["k_norm_g"][l], 2)
        for n in range(3):
            pv[:, L_CONV + 2 * n:L_CONV + 2 * n + 2] = by_part(g["conv_w"][l, n])
        pv[:, L_PSC:L_PSC + 2] = by_part(g["pool_scale"][l])
        pv[:, L_SINK:L_SINK + 16] = np.repeat(g["attn_sink"][l][heads], 2)[None]
        for n in range(4):
            r = 64 * (n % 2)
            ws[b + 1, r:r + 64, (n // 2) * P + r:(n // 2) * P + r + 64] = g["pool_w"][l, n]
        for n in range(2):
            ws[b + 1, :, T + n * P:T + (n + 1) * P] = g["peer_keys"][l, n].T
        ws[b + U_ADA:b + U_ADA + N_ADA] = tiles(g["w_ada"][l])
        w_in = g["w_in"][l]
        ws[b + U_IN:b + U_IN + N_IN] = tiles(np.concatenate([w_in[:, :512][:, perm], w_in[:, 512:]], 1))
        w_out = g["w_out"][l]
        ws[b + U_OUT:b + U_OUT + N_OUT] = tiles(np.concatenate([w_out[:512][perm], w_out[512:]], 0))
        ws[b + U_WQ:b + U_WQ + N_WQ] = tiles(g["peer_wq"][l])
        eu = g["peer_u"][l].reshape(P, P, KD, P).transpose(1, 3, 2, 0).reshape(P, P, D)
        ev = g["peer_v"][l].reshape(P, P, D).transpose(1, 0, 2)
        e = ws[b + U_EXP:b + PER_LAYER]
        e[0:2] = eu[0:2]
        mid = e[2:254].reshape(63, 4, P, D)
        mid[:, 0:2] = eu[2:].reshape(63, 2, P, D)
        mid[:, 2:4] = ev[:126].reshape(63, 2, P, D)
        e[254:256] = ev[126:128]
    s = ws[BASE2:]
    w_in2 = g["w_in_2"][0]
    s[V_IN:V_IN + N_IN2] = tiles(np.ascontiguousarray(w_in2[:, :N_IN2 * P]))
    wdt = w_in2[:, N_IN2 * P:].reshape(KD, P, 12).transpose(1, 0, 2)
    s[V_OUT:V_OUT + 8] = tiles(g["w_out_2"][0])
    s[V_XQ:V_XQ + 8] = tiles(g["xa_wq_2"][0])
    s[V_XK:V_XK + 8] = tiles(g["xa_wk_2"][0])
    s[V_XV:V_XV + 8] = g["xa_wv_2"][0].reshape(KD, P, D)
    s[V_XO:V_XO + 8] = tiles(g["xa_wo_2"][0])
    up = tiles(g["ffn_w_up_2"][0])
    dn = g["ffn_w_down_2"][0].reshape(N_FF, P, D)
    f = s[V_FFN:]
    f[0], f[1] = up[0], up[N_FF]
    mid = f[2:65].reshape(N_FF - 1, 3, P, D)
    mid[:, 0], mid[:, 1], mid[:, 2] = up[1:N_FF], up[N_FF + 1:], dn[:N_FF - 1]
    f[65] = dn[N_FF - 1]

    v2 = np.zeros((P, W_COLS), np.float32)

    def put(at, x):
        v2[:, at:at + x.shape[1]] = x

    for at, name in ((W_MIX, "mix_norm_w_2"), (W_XA, "xa_norm_w_2"), (W_MEM, "mem_norm_w_2"),
                     (W_FFN, "ffn_norm_w_2"), (W_SN, "ssd_norm_w_2"), (W_CB, "ssd_conv_b_2"),
                     (W_UD, "s5_d_2"), (W_FB, "ffn_conv_b_2")):
        put(at, by_part(g[name][0]))
    put(W_FIN, by_part(g["final_norm_w_2"]))
    put(W_CW, by_part(g["ssd_conv_w_2"][0]))
    put(W_FW, by_part(g["ffn_conv_w_2"][0]))
    put(W_SD, by_part(np.repeat(g["ssd_d_2"][0], 64)))
    put(W_LR, by_part(g["s5_lambda_re_2"][0].reshape(-1)))
    put(W_LI, by_part(g["s5_lambda_im_2"][0].reshape(-1)))
    put(W_DT, by_part(np.repeat(g["s5_log_dt_2"][0], 64)))
    put(W_DTB, np.repeat(g["ssd_dt_bias_2"][0][None], P, 0))
    put(W_ALOG, np.repeat(g["ssd_a_log_2"][0][None], P, 0))
    s5b = np.zeros((P, 2, 8, P), np.float32)
    s5c = np.zeros((P, 2, 8, P), np.float32)
    for n, part in enumerate(("re", "im")):
        for j in range(8):
            for q in range(2):
                grp = 2 * j + q
                r = 16 * (grp % 8)
                s5b[r:r + 16, n, j, 64 * q:64 * q + 64] = g[f"s5_b_{part}_2"][0, grp].T
                s5c[64 * q:64 * q + 64, n, j, r:r + 16] = g[f"s5_c_{part}_2"][0, grp].T

    def fm(x):
        return np.ascontiguousarray(x[0].T.reshape(KD, P, T).transpose(1, 0, 2))

    arrays = {
        "wstream": ws, "consts": tables(), "xT": fm(g["x"]), "memT": fm(g["mem_2"]),
        "cT": np.ascontiguousarray(by_part(g["c"][0])),
        "pos": np.ascontiguousarray(np.repeat(g["positions"], P, 0)),
        "vec2": v2, "s5b": s5b, "s5c": s5c,
        "wglu": np.ascontiguousarray(g["s5_w_glu_2"][0].reshape(2, P, T).transpose(1, 0, 2)),
        "wdt": np.ascontiguousarray(wdt),
    }
    nc = bacc.Bacc("TRN2", target_bir_lowering=False, num_devices=1, dynamic_dma_scratch_size=1024)
    args = [nc.dram_tensor(k, a.shape, mybir.dt.from_np(a.dtype), kind="ExternalInput").ap()
            for k, a in arrays.items()]
    args.append(nc.dram_tensor("outT", (P, KD, T), F32, kind="ExternalOutput").ap())
    program(nc, *args)
    r = run(nc, [arrays], core_ids=[0])
    return np.ascontiguousarray(r.results[0]["outT"].transpose(2, 1, 0).reshape(1, T, D))
```

```python
import math
from contextlib import ExitStack

import concourse.bass as bass
from concourse import mybir

ALU = mybir.AluOpType
ACT = mybir.ActivationFunctionType
F32 = mybir.dt.float32
F32R = mybir.dt.float32r
I32 = mybir.dt.int32
U32 = mybir.dt.uint32
AX_X = mybir.AxisListType.X

P = 128
T = 256
TT = T // P
D = 1024
KD = D // P
DEPTH = 2
EPS = 1e-6
NEG = -1e30

SLOTS = 8
HIGHS = 4
U_PARAMS, N_PARAMS = 0, 2
U_ADA, N_ADA = 2, 16
U_IN, N_IN = 18, 14
U_ADB, N_ADB = 32, 32
U_OUT, N_OUT = 64, 8
U_WQ, N_WQ = 72, 16
U_EXP, N_EXP = 88, 256
PER_LAYER = U_EXP + N_EXP
BASE2 = DEPTH * PER_LAYER
V_IN, N_IN2 = 0, 22
V_OUT = 22
V_XQ, V_XK, V_XV, V_XO = 30, 38, 46, 54
V_FFN, N_FF = 62, 22
UNITS2 = V_FFN + 3 * N_FF
UNITS = BASE2 + UNITS2
PAIRS = 64

L_N1, L_N2, L_BADA, L_QG, L_KG, L_CONV, L_PSC, L_SINK = 0, 8, 16, 64, 65, 66, 72, 74
L_COLS = 90
_at = 0


def _cols(n):
    global _at
    _at += n
    return _at - n


W_MIX, W_XA, W_MEM, W_FFN, W_FIN = (_cols(8) for _ in range(5))
W_CW, W_CB, W_SN, W_SD, W_UD = _cols(56), _cols(14), _cols(6), _cols(6), _cols(2)
W_FW, W_FB = _cols(66), _cols(22)
W_LR, W_LI, W_DT = _cols(8), _cols(8), _cols(8)
W_DTB, W_ALOG = _cols(12), _cols(12)
W_COLS = _at
_at = 0
C_ID, C_ONE, C_BLK, C_ROT, C_TRI, C_CAUS = (_cols(128) for _ in range(6))
C_IOTA, C_I16, C_INV = _cols(128), _cols(16), _cols(1)
C_COLS = _at
C_MASK, C_CNT = 0, 512


class Steps:

    def __init__(self, eng, sems):
        self.eng, self.sems, self.n = eng, sems, {}

    def mark(self, ins, name):
        self.n[name] = self.n.get(name, 0) + 1
        ins.then_inc(self.sems(name), 1)

    def __call__(self, ins, name):
        self.mark(ins, name)
        self.wait(name, self.n[name])

    def wait(self, name, value):
        self.eng.wait_ge(self.sems(name), value)


def program(nc, wstream, consts, mixconst, crow, xT, memT, pos, vec2, s5b, s5c, wglu, wdt, out):
    ctx = ExitStack()
    with ctx:
        def sb(name, shape, dt=F32):
            return ctx.enter_context(nc.sbuf_tensor(name, shape, dt))

        def two(name, shape):
            at = -(-nc.sbuf_base // 32) * 32
            t = sb(name, shape)
            return t, nc.alloc_sbuf_tensor_at(name + "_lo", shape, F32R, offset=at)

        arena_at = -(-nc.sbuf_base // 32) * 32
        AR = sb("arena", [P, P * T])

        def rounded(at, *shape):
            return nc.alloc_sbuf_tensor_at(f"part_at_{at}", [P, *shape], F32R, offset=arena_at + 4 * at)[:, :, :]

        RING, RING_LO = two("ring", [P, SLOTS, D])
        H, H_LO = two("normed", [P, KD, T])
        WK, WK_LO = two("work", [P, 2, D])
        HOT = nc.alloc_sbuf_tensor_at("one_hots", [P, HIGHS, D], F32, offset=-(-nc.sbuf_base // 32) * 32)
        RING_HI = sb("ring_hi", [P, HIGHS, D], F32R)
        H_HI = sb("normed_hi", [P, KD, T], F32R)
        X = sb("residual", [P, KD, T])
        CST = sb("consts_sb", [P, C_COLS])
        LV = sb("layer_vectors", [P, L_COLS])
        PK = sb("pool_and_keys", [P, 512])
        MOD = sb("modulation", [P, 48])
        S1G = sb("scale_gain", [P, 16])
        RS = sb("rstd", [P, 3, T])
        COSSIN = sb("rope", [P, 2, T])
        J = sb("routes", [P, 3, T])
        PS = ctx.enter_context(nc.psum_tensor("banks", [P, 8, 512], F32))

        loaded = [ctx.enter_context(nc.semaphore(f"loaded{i}")) for i in range(SLOTS)]
        units_used = ctx.enter_context(nc.semaphore("units_used"))
        pool_of = [ctx.enter_context(nc.semaphore(f"stage{i}")) for i in range(120)]
        named = {}

        def S(name):
            if name not in named:
                named[name] = pool_of[len(named)]
            return named[name]

        def end_of_block():
            nums = sorted(s.num for s in pool_of)
            assert nums[-1] - nums[0] == len(nums) - 1
            nc.gpsimd.sem_clear(range(nums[0], nums[-1] + 1))
            nc.all_engine_barrier()
            named.clear()

        def col(t, c):
            return t[:, c:c + 1]

        ident = CST[:, C_ID:C_ID + P]
        ones = CST[:, C_ONE:C_ONE + P]
        blk64 = CST[:, C_BLK:C_BLK + P]
        rot = CST[:, C_ROT:C_ROT + P]
        tri = CST[:, C_TRI:C_TRI + P]
        causal = CST[:, C_CAUS:C_CAUS + P]
        iota = CST[:, C_IOTA:C_IOTA + P]
        iota16 = CST[:, C_I16:C_I16 + 16]
        invf = CST[:, C_INV:C_INV + 1]

        class Arena:
            def __init__(self):
                self.at = 0

            def __call__(self, *shape, dt=F32):
                n = int(math.prod(shape))
                o, self.at = self.at, self.at + -(-n // 8) * 8
                assert self.at <= P * T
                if dt == F32R:
                    return rounded(o, *shape)
                v = AR[:, o:o + n]
                if dt != F32:
                    v = v.bitcast(dt)
                names = "abcd"[:len(shape)]
                if len(shape) == 1:
                    return v
                return v.rearrange(f"p ({' '.join(names)}) -> p {' '.join(names)}",
                                   **{k: s for k, s in zip(names[1:], shape[1:])})

            def split(self, *shape):
                here = self.at
                full = self(*shape)
                self.at = here
                return full, self(*shape, dt=F32R), self(*shape, dt=F32R)

        def stream(sp, base, u0, u1):
            def one(u, s):
                sp.wait_ge(units_used, u - (SLOTS - 1))
                sp.dma_start(RING[:, s, :], wstream[u]).then_inc(loaded[s], 16)
            n = (u1 - u0) // SLOTS
            if n > 1:
                with sp.Fori(0, n) as r:
                    for s in range(SLOTS):
                        one(r * SLOTS + (base + u0 + s), (u0 + s) % SLOTS)
                u0 += n * SLOTS
            for u in range(u0, u1):
                one(base + u, u % SLOTS)

        def arrived(eng, base, u):
            eng.wait_ge(loaded[u % SLOTS], base * (16 // SLOTS) + 16 * (u // SLOTS + 1))

        def used(base, u):
            return base + (u + 1)

        class Tiles:

            def __init__(self):
                self.n = 0

            def bank(self, pe):
                return self.bank_after(pe, "bank_emptied")

            def bank_after(self, pe, emptied):
                if self.n >= 4:
                    pe.wait_ge(S(emptied), self.n - 3)
                self.n += 1
                return 2 + (self.n - 1) % 4

            def linear(self, pe, base, u0, n, hi, lo, s0):
                for i in range(n):
                    b = self.bank(pe)
                    pe.wait_ge(S("split"), s0 + i + 1)
                    unit_product(pe, PS[:, b, 0:T], u0 + i, hi, lo).then_inc(units_used, 1)

        def parts_of(u):
            return RING_HI[:, u % HIGHS, :], RING_LO[:, u % SLOTS, :]

        def unit_product(pe, dst, u, hi, lo):
            w_hi, w_lo = parts_of(u)
            for k in range(KD):
                o = slice(k * P, (k + 1) * P)
                pe.matmul(dst, w_hi[:, o], hi[:, k, :], start=(k == 0), stop=False)
                pe.matmul(dst, w_hi[:, o], lo[:, k, :], start=False, stop=False)
                mm = pe.matmul(dst, w_lo[:, o], hi[:, k, :], start=False, stop=(k == KD - 1))
            return mm

        def unit_spread(pe, u, hi, lo, first, last):
            w_hi, w_lo = parts_of(u)
            for k in range(KD):
                o = slice(k * P, (k + 1) * P)
                dst = PS[:, 4 + k // 2, (k % 2) * T:(k % 2 + 1) * T]
                pe.matmul(dst, w_hi[:, o], hi, start=(first and k % 2 == 0), stop=False, skip_group_check=True)
                pe.matmul(dst, w_hi[:, o], lo, start=False, stop=False, skip_group_check=True)
                mm = pe.matmul(dst, w_lo[:, o], hi, start=False, stop=last, skip_group_check=True)
            return mm

        def split_high(act, base, u, fresh):
            arrived(act.eng, base, u)
            if not fresh:
                act.eng.wait_ge(units_used, base + (u - HIGHS + 1))
            act.mark(act.eng.activation(RING_HI[:, u % HIGHS, :], RING[:, u % SLOTS, :], ACT.Copy), "high")

        def split_low(v, u, n):
            v.wait("high", n + 1)
            v.mark(v.eng.tensor_tensor(RING_LO[:, u % SLOTS, :], RING[:, u % SLOTS, :],
                                       RING_HI[:, u % HIGHS, :].bitcast(F32), ALU.subtract), "split")

        def operand_high(act, hi, full, n, ready, name):
            for k in range(n):
                act.wait(ready, k + 1)
                act.mark(act.eng.activation(hi[:, k, :], full[:, k, :], ACT.Copy), name)

        def operand_low(v, lo, full, hi, n, name, done):
            for k in range(n):
                v.wait(name, k + 1)
                v.mark(v.eng.tensor_tensor(lo[:, k, :], full[:, k, :], hi[:, k, :].bitcast(F32), ALU.subtract), done)

        class Drain:

            def __init__(self, eng):
                self.eng, self.n = eng, 0

            def __call__(self):
                self.n += 1
                return 2 + (self.n - 1) % 4

        def norm_squares(act, src, sq, name):
            act(nc.scalar.activation(sq, src, ACT.Square), name + "_squares")

        def norm_sum(pe, sq, n, name, bank=1):
            pe.wait_ge(S(name + "_squares"), 1)
            for k in range(n):
                mm = pe.matmul(PS[:, bank, 0:T], ones, sq[:, k, :], start=(k == 0), stop=(k == n - 1))
            mm.then_inc(S(name + "_sum"), 1)

        def norm_inverse(v, width, name, bank=1):
            v.wait(name + "_sum", 1)
            v(nc.vector.tensor_scalar(RS[:, 0, :], PS[:, bank, 0:T], 1.0 / width, EPS, ALU.mult, ALU.add),
              name + "_var")
            v(nc.vector.reciprocal(RS[:, 1, :], RS[:, 0, :]), name + "_inverse")

        def norm_root(act, name):
            act.wait(name + "_inverse", 1)
            act(nc.scalar.activation(RS[:, 2, :], RS[:, 1, :], ACT.Sqrt), name + "_rstd")

        def norm_apply(v, dst, src, gain, shift, name):
            v.wait(name + "_rstd", 1)
            v(nc.vector.tensor_tensor(dst, src, RS[:, 2:3, :].to_broadcast([P, KD, T]), ALU.mult),
              name + "_scaled")
            for k in range(KD):
                if shift is None:
                    i = nc.vector.tensor_scalar(dst[:, k, :], dst[:, k, :], col(gain, k), None, ALU.mult)
                else:
                    i = nc.vector.tensor_scalar(dst[:, k, :], dst[:, k, :], col(gain, k), col(shift, k),
                                                ALU.mult, ALU.add)
                v.mark(i, name + "_applied")
            v.wait(name + "_applied", KD)

        def reduce_angle(v, r, a, t):
            v(nc.vector.tensor_scalar(t, a, 1.0 / (2 * math.pi), 12582912.0, ALU.mult, ALU.add), "angle")
            v(nc.vector.tensor_scalar(t, t, -12582912.0, None, ALU.add), "angle")
            src = a
            for c in (6.28125, 0.00193405151367187500, 2 * math.pi - 6.28125 - 0.00193405151367187500):
                v(nc.vector.scalar_tensor_tensor(r, t, -c, src, ALU.mult, ALU.add), "angle")
                src = r
            v(nc.vector.tensor_scalar(r, r, -3.1415925, 3.1415925, ALU.max, ALU.min), "angle")

        def quarter_turn(v, r2, r, t):
            v(nc.vector.tensor_scalar(r2, r, math.pi / 2, None, ALU.add), "angle")
            v(nc.vector.tensor_scalar(t, r2, math.pi, -2 * math.pi, ALU.is_gt, ALU.mult), "angle")
            v(nc.vector.tensor_tensor(r2, r2, t, ALU.add), "angle")
            v(nc.vector.tensor_scalar(r2, r2, -3.1415925, 3.1415925, ALU.max, ALU.min), "angle")

        a0 = Arena()
        posi, posf, ang, tmp, red, red2 = a0(T, dt=I32), a0(T), a0(T), a0(T), a0(T), a0(T)
        with nc.Block() as block:
            @block.sync
            def _(sp):
                sp.dma_start(CST[:, :], consts).then_inc(S("inputs"), 16)
                sp.dma_start(X[:, :, :], xT).then_inc(S("inputs"), 16)
                sp.dma_start(posi, pos).then_inc(S("inputs"), 16)
                for u in range(SLOTS):
                    sp.dma_start(RING[:, u, :], wstream[u]).then_inc(loaded[u], 16)

            @block.vector
            def _(dve):
                v = Steps(dve, S)
                v.wait("inputs", 48)
                v(dve.tensor_copy(posf, posi), "pos")
                v(dve.tensor_scalar(ang, posf, invf, None, ALU.mult), "pos")
                reduce_angle(v, red, ang, tmp)
                quarter_turn(v, red2, red, tmp)

            @block.scalar
            def _(sc):
                act = Steps(sc, S)
                act.wait("angle", 10)
                act(sc.activation(COSSIN[:, 0, :], red2, ACT.Sin), "tables")
                act(sc.activation(COSSIN[:, 1, :], red, ACT.Sin), "tables")
        end_of_block()

        at = {}
        with nc.Fori(0, DEPTH) as layer:
            base = layer * PER_LAYER

            a = Arena()
            CROW = a(D)
            MASK = a(512)
            INV_CNT = a(2, T)
            Z = a(14, T)
            SQ = a(KD, T)
            QSQ, QVAR, QN, QR, QT = (a(5, T) for _ in range(5))
            SC = a(16, T)
            MX, NMX, ESK, SUM = a(16), a(16), a(16), a(16)
            PT = a(8, 2, T)
            VP = a(2, 2, P)
            CU = a(2, T + 2)
            CY = a(2, T)
            PU, P2, P4, P8, P16 = (a(2, T + 16) for _ in range(5))
            PL = a(2, T)
            MIX, MIX_LO, MIX_HI = a.split(8, T)
            with nc.Block() as block:
                @block.sync
                def _(sp):
                    sp.dma_start(CROW, crow).then_inc(S("c_row"), 16)
                    sp.dma_start(AR[:, D:2 * D], mixconst).then_inc(S("mix_consts"), 16)
                    stream(sp, base, SLOTS, U_WQ + SLOTS)

                @block.gpsimd
                def _(pool):
                    pool.memset(VP, 0.0).then_inc(S("cleared"), 1)
                    pool.memset(CU, 0.0).then_inc(S("cleared"), 1)
                    pool.memset(PU, 0.0).then_inc(S("cleared"), 1)

                @block.tensor
                def _(pe):
                    pe.wait_ge(units_used, base + N_PARAMS)
                    norm_sum(pe, SQ, KD, "n1")
                    pe.wait_ge(S("h_low"), KD)
                    tiles = Tiles()
                    tiles.linear(pe, base, U_IN, N_IN, H_HI, H_LO, 0)
                    pe.wait_ge(S("qk_squares"), 1)
                    for i in range(5):
                        b = tiles.bank(pe)
                        pe.matmul(PS[:, b, 0:T], blk64, QSQ[:, i, :], start=True, stop=True)\
                            .then_inc(S("qk_sums"), 1)
                    pe.wait_ge(S("qk_normed"), 2)
                    for i in range(5):
                        b = tiles.bank(pe)
                        pe.matmul(PS[:, b, 0:T], rot, QN[:, i, :], start=True, stop=True)\
                            .then_inc(S("qk_rotated"), 1)
                    b = tiles.bank(pe)
                    for kt in range(TT):
                        mm = pe.transpose(PS[:, b, kt * P:(kt + 1) * P], Z[:, 5, kt * P:(kt + 1) * P], ident)
                    mm.then_inc(S("v_turned"), 1)
                    pe.wait_ge(S("qk_roped"), 1)
                    for hh in range(8):
                        j, half = hh // 2, hh % 2
                        rows = slice(64 * half, 64 * half + 64)
                        b = tiles.bank(pe)
                        for qt in range(TT):
                            mm = pe.matmul(PS[:, b, qt * T:(qt + 1) * T], QR[rows, j, qt * P:(qt + 1) * P],
                                           QR[rows, 4, :], start=True, stop=True)
                        mm.then_inc(S("scored"), 1)
                    pe.wait_ge(S("pooled"), 1)
                    for i in range(2):
                        b = tiles.bank(pe)
                        pe.matmul(PS[:, b, 0:T], PK[:, i * P:(i + 1) * P], PL[:, i, :], start=True, stop=True)\
                            .then_inc(S("pool_mixed"), 1)
                    at["pool"] = tiles.n
                    pe.wait_ge(S("probs"), 1)
                    for hh in range(8):
                        b = tiles.bank(pe)
                        for kt in range(TT):
                            for qt in range(TT):
                                mm = pe.transpose(PS[:, b, kt * T + qt * P:kt * T + (qt + 1) * P],
                                                  SC[:, 2 * hh + qt, kt * P:(kt + 1) * P], ident)
                        mm.then_inc(S("probs_turned"), 1)
                    at["attended"] = tiles.n
                    pe.wait_ge(S("v_padded"), 1)
                    pe.wait_ge(S("bank_emptied"), tiles.n)
                    for j in range(4):
                        b = tiles.bank(pe)
                        for n in range(4):
                            half, kt = n // 2, n % 2
                            mm = pe.matmul(PS[:, b, 0:T], VP[:, kt, half, :], PT[:, 2 * j + half, kt, :],
                                           start=(n == 0), stop=(n == 3))
                        mm.then_inc(S("attended"), 1)
                    pe.wait_ge(S("conv_mixed"), 2)
                    pe.wait_ge(S("bank_emptied"), tiles.n)
                    pe.wait_ge(S("mix_low"), 5)
                    tiles.linear(pe, base, U_OUT, N_OUT, MIX_HI, MIX_LO, N_IN)

                @block.scalar
                def _(sc):
                    act = Steps(sc, S)
                    arrived(sc, base, 0)
                    sc.activation(LV[:, :], RING[:, 0, 0:L_COLS], ACT.Copy).then_inc(units_used, 1)
                    arrived(sc, base, 1)
                    sc.activation(PK[:, :], RING[:, 1, 0:512], ACT.Copy).then_inc(units_used, 1)
                    norm_squares(act, X[:, :, :], SQ, "n1")
                    norm_root(act, "n1")
                    act.wait("c_row", 16)
                    act(sc.activation(CROW, CROW, ACT.Silu), "c_act")
                    for i in range(HIGHS):
                        split_high(act, base, U_IN + i, True)
                    operand_high(act, H_HI, H, KD, "n1_applied", "h_high")
                    nxt = Drain(sc)
                    for i in range(N_IN):
                        sc.wait_ge(units_used, used(base, U_IN + i))
                        b = nxt()
                        act.mark(sc.activation(Z[:, i, :], PS[:, b, 0:T], ACT.Copy), "bank_emptied")
                        if i + HIGHS < N_IN:
                            split_high(act, base, U_IN + i + HIGHS, False)
                    act.wait("bank_emptied", N_IN)
                    act(sc.activation(QSQ, Z[:, 0:5, :], ACT.Square), "qk_squares")
                    act.wait("qk_inverse", 1)
                    act(sc.activation(QVAR, QVAR, ACT.Sqrt), "qk_rstd")
                    act.wait("maxes", 2)
                    act(sc.activation(ESK, ESK, ACT.Exp), "sink_exp")
                    for i in range(16):
                        act.mark(sc.activation(SC[:, i, :], SC[:, i, :], ACT.Exp, bias=NMX[:, i:i + 1],
                                               accum_out=SUM[:, i:i + 1]), "exps")
                    for i in range(HIGHS):
                        split_high(act, base, U_OUT + i, False)
                    act.wait("conv_mixed", 2)
                    act.wait("bank_emptied", at["pool"])
                    act.mark(sc.activation(MIX_HI[:, 4:8, :], MIX[:, 4:8, :], ACT.Copy), "mix_high")
                    for j in range(4):
                        act.wait("bank_emptied", at["attended"] + j + 1)
                        act.mark(sc.activation(MIX_HI[:, j, :], MIX[:, j, :], ACT.Copy), "mix_high")
                    for i in range(HIGHS, N_OUT):
                        split_high(act, base, U_OUT + i, False)

                @block.vector
                def _(dve):
                    v = Steps(dve, S)
                    dve.wait_ge(units_used, base + N_PARAMS)
                    norm_inverse(v, D, "n1")
                    v.wait("c_act", 1)

                    def modulation(u0, n, c):
                        for i in range(n):
                            u = u0 + i
                            arrived(dve, base, u)
                            dve.tensor_tensor_reduce(RING[:, u % SLOTS, :], RING[:, u % SLOTS, :], CROW, 1.0, 0.0,
                                                     ALU.mult, ALU.add, MOD[:, c + i:c + i + 1])\
                                .then_inc(units_used, 1)

                    modulation(U_ADA, N_ADA, 0)
                    dve.wait_ge(units_used, used(base, U_ADA + N_ADA - 1))
                    v(dve.tensor_tensor(MOD[:, 0:16], MOD[:, 0:16], LV[:, L_BADA:L_BADA + 16], ALU.add), "mod")
                    v(dve.tensor_scalar(S1G[:, 0:8], MOD[:, 8:16], 1.0, None, ALU.add), "mod")
                    v(dve.tensor_tensor(S1G[:, 0:8], S1G[:, 0:8], LV[:, L_N1:L_N1 + 8], ALU.mult), "mod")
                    for i in range(HIGHS):
                        split_low(v, U_IN + i, i)
                    norm_apply(v, H[:, :, :], X[:, :, :], S1G[:, 0:8], MOD[:, 0:8], "n1")
                    operand_low(v, H_LO, H, H_HI, KD, "h_high", "h_low")
                    for i in range(HIGHS, N_IN):
                        split_low(v, U_IN + i, i)
                    dve.wait_ge(units_used, used(base, U_IN + N_IN - 1))
                    modulation(U_ADB, 3, 16)
                    nxt = Drain(dve)
                    nxt.n = N_IN
                    v.n["bank_emptied"] = N_IN
                    for i in range(5):
                        v.wait("qk_sums", i + 1)
                        v(dve.tensor_scalar(QVAR[:, i, :], PS[:, nxt(), 0:T], 1.0 / 64, EPS, ALU.mult, ALU.add),
                          "bank_emptied")
                    v(dve.reciprocal(QVAR, QVAR), "qk_inverse")
                    modulation(U_ADB + 3, 2, 19)
                    v.wait("qk_rstd", 1)
                    v(dve.scalar_tensor_tensor(QN[:, 0:4, :], Z[:, 0:4, :], LV[:, L_QG:L_QG + 1], QVAR[:, 0:4, :],
                                               ALU.mult, ALU.mult), "qk_normed")
                    v(dve.scalar_tensor_tensor(QN[:, 4, :], Z[:, 4, :], LV[:, L_KG:L_KG + 1], QVAR[:, 4, :],
                                               ALU.mult, ALU.mult), "qk_normed")
                    v(dve.tensor_tensor(QR, QN, COSSIN[:, 0:1, :].to_broadcast([P, 5, T]), ALU.mult), "qk_cos")
                    modulation(U_ADB + 5, 1, 21)
                    for i in range(5):
                        v.wait("qk_rotated", i + 1)
                        v(dve.tensor_tensor(QT[:, i, :], PS[:, nxt(), 0:T], COSSIN[:, 1, :], ALU.mult),
                          "bank_emptied")
                    v(dve.tensor_tensor(QR, QR, QT, ALU.add), "qk_roped")
                    v.wait("v_turned", 1)
                    v.wait("cleared", 3)
                    b = nxt()
                    vt = PS[:, b, 0:T].rearrange("p (k h d) -> p k h d", k=2, h=2)
                    v(dve.tensor_copy(VP[:, :, 0, 0:64], vt[:, :, 0, :]), "v_padded")
                    v(dve.tensor_copy(VP[:, :, 1, 64:128], vt[:, :, 1, :]), "bank_emptied")
                    v.wait("mix_consts", 16)
                    modulation(U_ADB + 6, 2, 22)
                    for hh in range(8):
                        v.wait("scored", hh + 1)
                        v(dve.scalar_tensor_tensor(SC[:, 2 * hh:2 * hh + 2, :].rearrange("p a b -> p (a b)"),
                                                   PS[:, nxt(), :], 0.125, MASK, ALU.mult, ALU.add), "bank_emptied")
                    v(dve.tensor_reduce(MX, SC, AX_X, ALU.max), "max")
                    v(dve.tensor_tensor(MX, MX, LV[:, L_SINK:L_SINK + 16], ALU.max), "max")
                    v(dve.tensor_scalar(NMX, MX, -1.0, None, ALU.mult), "maxes")
                    v(dve.tensor_tensor(ESK, LV[:, L_SINK:L_SINK + 16], MX, ALU.subtract), "maxes")
                    v(dve.tensor_tensor(CU[:, :, 1:T + 1], Z[:, 10:12, :], Z[:, 6:8, :], ALU.mult), "conv")
                    for i in range(2):
                        w = [LV[:, L_CONV + 2 * n + i:L_CONV + 2 * n + i + 1] for n in range(3)]
                        v(dve.tensor_scalar(CY[:, i, :], CU[:, i, 0:T], w[0], None, ALU.mult), "conv")
                        for n in (1, 2):
                            v(dve.scalar_tensor_tensor(CY[:, i, :], CU[:, i, n:n + T], w[n], CY[:, i, :],
                                                       ALU.mult, ALU.add), "conv")
                        v(dve.tensor_tensor(MIX[:, 4 + i, :], CY[:, i, :], Z[:, 8 + i, :], ALU.mult), "conv_mixed")
                    v(dve.tensor_copy(PU[:, :, 8:8 + T], Z[:, 12:14, :]), "pool")
                    for dst, src, lo, m, n in ((P2, PU, 1, 1, 0), (P4, P2, 2, 1, 1), (P8, P4, 4, 2, 2),
                                               (P16, P8, 8, 4, 4)):
                        hi = T + 16 - lo
                        v(dve.tensor_tensor(dst[:, :, lo:hi], src[:, :, lo - m:hi - m], src[:, :, lo + n:hi + n],
                                            ALU.add), "pool")
                    for g, src in enumerate((P2, P4, P8, P16)):
                        r = slice(64 * (g % 2), 64 * (g % 2) + 64)
                        v(dve.tensor_tensor(PL[r, g // 2, :], src[r, g // 2, 8:8 + T], INV_CNT[r, g // 2, :],
                                            ALU.mult), "pool")
                    v(dve.tensor_tensor(PL, PL, Z[:, 12:14, :], ALU.subtract), "pooled")
                    for i in range(2):
                        v.wait("pool_mixed", i + 1)
                        v(dve.tensor_scalar(MIX[:, 6 + i, :], PS[:, nxt(), 0:T], LV[:, L_PSC + i:L_PSC + i + 1],
                                            None, ALU.mult), "bank_emptied")
                    modulation(U_ADB + 8, 16, 24)
                    v.wait("exps", 16)
                    v.wait("sink_exp", 1)
                    v(dve.tensor_tensor(SUM, SUM, ESK, ALU.add), "soft")
                    v(dve.reciprocal(SUM, SUM), "soft")
                    v(dve.tensor_tensor(SC, SC, SUM.unsqueeze(2).to_broadcast([P, 16, T]), ALU.mult), "probs")
                    for hh in range(8):
                        modulation(U_ADB + 24 + hh, 1, 40 + hh)
                        v.wait("probs_turned", hh + 1)
                        v(dve.tensor_copy(PT[:, hh, :, :].rearrange("p a b -> p (a b)"), PS[:, nxt(), :]),
                          "bank_emptied")
                    dve.wait_ge(units_used, used(base, U_ADB + N_ADB - 1))
                    v(dve.tensor_tensor(MOD[:, 16:48], MOD[:, 16:48], LV[:, L_BADA + 16:L_BADA + 48], ALU.add), "mod")
                    v(dve.tensor_scalar(S1G[:, 8:16], MOD[:, 32:40], 1.0, None, ALU.add), "mod")
                    v(dve.tensor_tensor(S1G[:, 8:16], S1G[:, 8:16], LV[:, L_N2:L_N2 + 8], ALU.mult), "mod")
                    for i in range(HIGHS):
                        split_low(v, U_OUT + i, N_IN + i)
                    for j in range(4):
                        v.wait("attended", j + 1)
                        v(dve.tensor_copy(MIX[:, j, :], PS[:, nxt(), 0:T]), "bank_emptied")
                    v.wait("mix_high", 1)
                    v.mark(dve.tensor_tensor(MIX_LO[:, 4:8, :], MIX[:, 4:8, :], MIX_HI[:, 4:8, :].bitcast(F32),
                                             ALU.subtract), "mix_low")
                    for j in range(4):
                        v.wait("mix_high", j + 2)
                        v.mark(dve.tensor_tensor(MIX_LO[:, j, :], MIX[:, j, :], MIX_HI[:, j, :].bitcast(F32),
                                                 ALU.subtract), "mix_low")
                    for i in range(N_OUT):
                        if i + HIGHS < N_OUT:
                            split_low(v, U_OUT + i + HIGHS, N_IN + i + HIGHS)
                        dve.wait_ge(units_used, used(base, U_OUT + i))
                        v.mark(dve.scalar_tensor_tensor(X[:, i, :], PS[:, nxt(), 0:T], col(MOD[:, 16:24], i),
                                                        X[:, i, :], ALU.mult, ALU.add), "bank_emptied")
                    v.wait("bank_emptied", nxt.n)
            end_of_block()

            a = Arena()
            SQ = a(KD, T)
            Q = a(16, T)
            KS = a(32, P)
            V16 = a(32, 16)
            I16 = a(32, 16, dt=U32)
            I16F = a(32, 16)
            CAND = a(16, 16, 16)
            TOP = a(16, 16)
            POS, PA, PB = a(16, 16, dt=U32), a(16, 16, dt=U32), a(16, 16, dt=U32)
            AF, BF = a(T), a(T)
            OH = a(T, 16)
            SEL = a(2, T)
            GT = a(16, 16)
            GS = a(16)
            PICK = a(3, T)
            with nc.Block() as block:
                @block.sync
                def _(sp):
                    stream(sp, base, U_WQ + SLOTS, U_EXP + SLOTS)

                @block.tensor
                def _(pe):
                    norm_sum(pe, SQ, KD, "n2")
                    pe.wait_ge(S("h_low"), KD)
                    tiles = Tiles()

                    def keys(h):
                        pe.wait_ge(S("q_copied"), 2 * h + 2)
                        if h >= 2:
                            pe.wait_ge(S("keys_copied"), h - 1)
                        for m in range(4):
                            tt, half = m // 2, m % 2
                            mm = pe.matmul(PS[:, h % 2, m * P:(m + 1) * P], Q[:, 2 * h + half, tt * P:(tt + 1) * P],
                                           PK[:, T + half * P:T + (half + 1) * P], start=True, stop=True)
                        mm.then_inc(S("key_scored"), 1)

                    for h in range(8):
                        for i in (2 * h, 2 * h + 1):
                            b = tiles.bank_after(pe, "q_copied")
                            pe.wait_ge(S("split"), i + 1)
                            unit_product(pe, PS[:, b, 0:T], U_WQ + i, H_HI, H_LO).then_inc(units_used, 1)
                        if h >= 1:
                            keys(h - 1)
                    keys(7)
                    tiles.n = 0
                    for i in range(3):
                        pe.wait_ge(S("by_tile"), i + 1)
                        b = tiles.bank(pe)
                        for tt in range(TT):
                            mm = pe.transpose(PS[:, b, tt * P:(tt + 1) * P], PICK[:, i, tt * P:(tt + 1) * P], ident)
                        mm.then_inc(S("routes_turned"), 1)

                @block.scalar
                def _(sc):
                    act = Steps(sc, S)
                    norm_squares(act, X[:, :, :], SQ, "n2")
                    norm_root(act, "n2")
                    for i in range(HIGHS):
                        split_high(act, base, U_WQ + i, True)
                    operand_high(act, H_HI, H, KD, "n2_applied", "h_high")
                    nxt = Drain(sc)

                    def keys(h):
                        act.wait("key_scored", h + 1)
                        act.mark(sc.activation(KS[:, 4 * h:4 * h + 4, :].rearrange("p a b -> p (a b)"),
                                               PS[:, h % 2, :], ACT.Copy), "keys_copied")

                    for i in range(N_WQ):
                        sc.wait_ge(units_used, used(base, U_WQ + i))
                        act.mark(sc.activation(Q[:, i, :], PS[:, nxt(), 0:T], ACT.Copy), "q_copied")
                        if i + HIGHS < N_WQ:
                            split_high(act, base, U_WQ + i + HIGHS, False)
                        if i % 2 and i >= 3:
                            keys(i // 2 - 1)
                    keys(7)
                    nxt.n = 0
                    act.wait("centred", 1)
                    act(sc.activation(GT, GT, ACT.Exp), "gate_exp")
                    for i, src in enumerate((SEL[:, 0, :], SEL[:, 1, :], GT.rearrange("p a b -> p (a b)"))):
                        act.wait("routed", i + 1)
                        act.mark(sc.activation(PICK[:, i, :].rearrange("p (t h k) -> p h t k", h=8, t=TT),
                                               src.rearrange("p (h t k) -> p h t k", h=8, t=TT), ACT.Copy),
                                 "by_tile")
                    for i in range(3):
                        act.wait("routes_turned", i + 1)
                        act.mark(sc.activation(J[:, i, :], PS[:, nxt(), 0:T], ACT.Copy), "bank_emptied")
                    act.wait("bank_emptied", nxt.n)

                @block.vector
                def _(dve):
                    v = Steps(dve, S)
                    norm_inverse(v, D, "n2")
                    for i in range(HIGHS):
                        split_low(v, U_WQ + i, i)
                    norm_apply(v, H[:, :, :], X[:, :, :], S1G[:, 8:16], MOD[:, 24:32], "n2")
                    operand_low(v, H_LO, H, H_HI, KD, "h_high", "h_low")

                    def top16(rows, src, val, idx):
                        for half in range(2):
                            o = slice(8 * half, 8 * half + 8)
                            for r in rows:
                                v.mark(dve.max(val[:, r, o], src(r)), "top")
                            v.wait("top", v.n["top"])
                            for r in rows:
                                v.mark(dve.max_index(idx[:, r, o], val[:, r, o], src(r)), "top")
                            if half == 0:
                                for r in rows:
                                    v.mark(dve.match_replace(src(r), val[:, r, o], src(r), -3e38), "top")
                            v.wait("top", v.n["top"])

                    for h in range(8):
                        for i in (2 * h, 2 * h + 1):
                            if i + HIGHS < N_WQ:
                                split_low(v, U_WQ + i + HIGHS, i + HIGHS)
                        if h >= 1:
                            v.wait("keys_copied", h)
                            top16(range(4 * h - 4, 4 * h), lambda r: KS[:, r, :], V16, I16)
                    v.wait("keys_copied", 8)
                    top16(range(28, 32), lambda r: KS[:, r, :], V16, I16)
                    v(dve.tensor_copy(I16F, I16), "pick")
                    pair = V16.rearrange("p (g h) k -> p g h k", h=2)
                    v(dve.tensor_tensor(CAND, pair[:, :, 0, :].unsqueeze(3).to_broadcast([P, 16, 16, 16]),
                                        pair[:, :, 1, :].unsqueeze(2).to_broadcast([P, 16, 16, 16]), ALU.add), "pick")
                    flat = CAND.rearrange("p g i j -> p g (i j)")
                    top16(range(16), lambda r: flat[:, r, :], TOP, POS)
                    v(dve.tensor_tensor(GT, TOP, TOP[:, :, 0:1].to_broadcast([P, 16, 16]), ALU.subtract), "centred")
                    v(dve.tensor_scalar(PA, POS, 4, None, ALU.logical_shift_right), "pick")
                    v(dve.tensor_scalar(PB, POS, 15, None, ALU.bitwise_and), "pick")
                    ipair = I16F.rearrange("p (g h) k -> p g h k", h=2)
                    for n, (pi, pf) in enumerate(((PA, AF), (PB, BF))):
                        v(dve.tensor_copy(pf, pi.rearrange("p a b -> p (a b)")), "pick")
                        v(dve.tensor_tensor(OH, pf.unsqueeze(2).to_broadcast([P, T, 16]),
                                            iota16.unsqueeze(1).to_broadcast([P, T, 16]), ALU.is_equal), "pick")
                        oh4 = OH.rearrange("p (g k) j -> p g k j", g=16)
                        v(dve.tensor_tensor(oh4, oh4, ipair[:, :, n, :].unsqueeze(2).to_broadcast([P, 16, 16, 16]),
                                            ALU.mult), "pick")
                        v(dve.tensor_reduce(SEL[:, n, :], OH, AX_X, ALU.add), "routed")
                    v.wait("gate_exp", 1)
                    v(dve.tensor_reduce(GS, GT, AX_X, ALU.add), "gate")
                    v(dve.reciprocal(GS, GS), "gate")
                    v(dve.tensor_tensor(GT, GT, GS.unsqueeze(2).to_broadcast([P, 16, 16]), ALU.mult), "routed")
            end_of_block()

            G = AR[:, :].rearrange("p (i t) -> p i t", i=P)
            hot = HOT[:, :, :].rearrange("p s (m t i) -> p s m t i", m=2, t=4)
            with nc.Block() as block:
                def groups(eng, body):
                    for s in range(HIGHS):
                        body(s, s, True)
                    with eng.Fori(1, T // 4 // HIGHS) as r:
                        for s in range(HIGHS):
                            body(r * HIGHS + s, s, False)

                @block.vector
                def _(dve):
                    def body(g, s, first):
                        if not first:
                            dve.wait_ge(S("g_made"), g - HIGHS + 1)
                        dve.tensor_tensor(hot[:, s], J[:, 0:2, bass.ds(g * 4, 4)].unsqueeze(3)
                                          .to_broadcast([P, 2, 4, P]),
                                          iota.unsqueeze(1).unsqueeze(1).to_broadcast([P, 2, 4, P]), ALU.is_equal)\
                            .then_inc(S("one_hots"), 1)
                    groups(dve, body)

                @block.gpsimd
                def _(pool):
                    def body(g, s, first):
                        pool.wait_ge(S("one_hots"), g + 1)
                        pool.tensor_tensor(hot[:, s, 1], hot[:, s, 1],
                                           J[:, 2, bass.ds(g * 4, 4)].unsqueeze(2).to_broadcast([P, 4, P]),
                                           ALU.mult).then_inc(S("gated"), 1)
                    groups(pool, body)

                @block.tensor
                def _(pe):
                    def body(g, s, first):
                        pe.wait_ge(S("gated"), g + 1)
                        if not first:
                            pe.wait_ge(S("g_copied"), g - HIGHS + 1)
                        for t in range(4):
                            mm = pe.matmul(PS[:, s, t * P:(t + 1) * P], hot[:, s, 0, t, :], hot[:, s, 1, t, :],
                                           start=True, stop=True)
                        mm.then_inc(S("g_made"), 1)
                    groups(pe, body)

                @block.scalar
                def _(sc):
                    def body(g, s, first):
                        sc.wait_ge(S("g_made"), g + 1)
                        sc.activation(G[:, :, bass.ds(g * 4, 4)],
                                      PS[:, s, :].rearrange("p (t i) -> p i t", t=4), ACT.Copy)\
                            .then_inc(S("g_copied"), 1)
                    groups(sc, body)
                    sc.wait_ge(S("g_copied"), T // 4)
            end_of_block()

            with nc.Block() as block:
                E, E_LO, E_HI = WK[:, :, 0:512], WK_LO[:, :, 0:512], WK_LO[:, :, 512:1024]

                @block.sync
                def _(sp):
                    stream(sp, base, U_EXP + SLOTS, PER_LAYER + SLOTS)

                @block.tensor
                def _(pe):
                    def first_product(i, r, bank):
                        for e in range(2):
                            pe.wait_ge(S("split"), r * SLOTS + (i + e + 1))
                            unit_product(pe, PS[:, bank, e * T:(e + 1) * T], i + e, H_HI, H_LO)\
                                .then_inc(units_used, 1)

                    def second_product(i, r, s, j, first=False, last=False):
                        pe.wait_ge(S("gated"), j + 1)
                        for e in range(2):
                            pe.wait_ge(S("split"), r * SLOTS + (i + e + 1))
                            o = slice(e * T, (e + 1) * T)
                            unit_spread(pe, i + e, E_HI[:, s, o], E_LO[:, s, o], first and e == 0, last and e == 1)\
                                .then_inc(units_used, 1)

                    def step(r, q, peeled):
                        j = r * 2 + q
                        if not (peeled and q == 0):
                            pe.wait_ge(S("gelu_done"), j)
                        first_product(2 + 4 * q, r, 1 - q)
                        second_product(4 + 4 * q, r, q, j, first=peeled and q == 0)

                    first_product(0, 0, 0)
                    step(0, 0, True)
                    step(0, 1, True)
                    with pe.Fori(1, 31) as r:
                        step(r, 0, False)
                        step(r, 1, False)
                    step(31, 0, False)
                    second_product(6, 31, 1, 63, last=True)

                @block.scalar
                def _(sc):
                    def high(i, r, fresh=False):
                        sc.wait_ge(loaded[i % SLOTS], (base + U_EXP) * 2 + 16 * (i // SLOTS + 1) + 16 * r)
                        if not fresh:
                            sc.wait_ge(units_used, base + r * SLOTS + (U_EXP + i - HIGHS + 1))
                        sc.activation(RING_HI[:, i % HIGHS, :], RING[:, i % SLOTS, :], ACT.Copy)\
                            .then_inc(S("high"), 1)

                    def step(r, q, first=False):
                        j, i = r * 2 + q, 4 * q
                        high(2 + i, r, first)
                        sc.wait_ge(units_used, base + U_EXP + (2 if first else r * SLOTS + i))
                        sc.activation(E[:, q, :], PS[:, q, :], ACT.Gelu).then_inc(S("gelu_done"), 1)
                        high(3 + i, r, first)
                        high(4 + i, r)
                        sc.wait_ge(S("weighted"), j + 1)
                        sc.activation(E_HI[:, q, :], E[:, q, :], ACT.Copy).then_inc(S("e_high"), 1)
                        high(5 + i, r)

                    high(0, 0, True)
                    high(1, 0, True)
                    step(0, 0, True)
                    step(0, 1)
                    with sc.Fori(1, 31) as r:
                        step(r, 0)
                        step(r, 1)
                    step(31, 0)
                    high(6, 31)
                    sc.wait_ge(units_used, base + U_EXP + 252)
                    sc.activation(E[:, 1, :], PS[:, 1, :], ACT.Gelu).then_inc(S("gelu_done"), 1)
                    high(7, 31)
                    sc.wait_ge(S("weighted"), 64)
                    sc.activation(E_HI[:, 1, :], E[:, 1, :], ACT.Copy).then_inc(S("e_high"), 1)

                @block.vector
                def _(dve):
                    def low(i, r):
                        dve.wait_ge(S("high"), r * SLOTS + (i + 1))
                        dve.tensor_tensor(RING_LO[:, i % SLOTS, :], RING[:, i % SLOTS, :],
                                          RING_HI[:, i % HIGHS, :].bitcast(F32), ALU.subtract).then_inc(S("split"), 1)

                    def weight(j, s):
                        dve.wait_ge(S("gelu_done"), j + 1)
                        dve.tensor_tensor(E[:, s, :], E[:, s, :],
                                          G[:, bass.ds(j * 2, 2), :].rearrange("p a b -> p (a b)"), ALU.mult)\
                            .then_inc(S("weighted"), 1)

                    def rest(j, s):
                        dve.wait_ge(S("e_high"), j + 1)
                        dve.tensor_tensor(E_LO[:, s, :], E[:, s, :], E_HI[:, s, :].bitcast(F32), ALU.subtract)\
                            .then_inc(S("gated"), 1)

                    def step(r, q):
                        j, i = r * 2 + q, 4 * q
                        low(2 + i, r)
                        weight(j, q)
                        low(3 + i, r)
                        low(4 + i, r)
                        rest(j, q)
                        low(5 + i, r)

                    low(0, 0)
                    low(1, 0)
                    with dve.Fori(0, 31) as r:
                        step(r, 0)
                        step(r, 1)
                    step(31, 0)
                    low(6, 31)
                    weight(63, 1)
                    low(7, 31)
                    rest(63, 1)
                    dve.wait_ge(units_used, base + PER_LAYER)
                    for k in range(KD):
                        i = dve.scalar_tensor_tensor(X[:, k, :], PS[:, 4 + k // 2, (k % 2) * T:(k % 2 + 1) * T],
                                                     MOD[:, 40 + k:41 + k], X[:, k, :], ALU.mult, ALU.add)
                    i.then_inc(S("x_done"), 1)
                    dve.wait_ge(S("x_done"), 1)
            end_of_block()

        base = BASE2
        a = Arena()
        V2 = a(W_COLS)
        SB = a(2, 8, P)
        SCM = a(2, 8, P)
        GLU = a(2, T)
        WDT = a(KD, 12)
        keep = a.at
        ZU = a(8, T)
        here = a.at
        XP = a(14, T + 3)
        there, a.at = a.at, here
        SYQ = a(6, T)
        mix_at = a.at
        MIX = a(8, T)
        a.at = max(a.at, there)
        XC = a(14, T)
        S1, S2, S3, S4 = a(24), a(24), a(24), a(24)
        DTM, DA, ACS, LAST, NEGA = a(2, 12), a(2, 12), a(2, 12), a(2, 12), a(12)
        DEC = a(12)
        here = seg_at = a.at
        SEG = a(2, 12, P)
        there, a.at = a.at, here
        SQ = a(KD, T)
        a.at = there
        ER1 = a(12, P)
        CB = a(4, 384)
        m_at = a.at
        M = a(12, 384)
        XD = a(2, 12, P)
        C8 = [a(8) for _ in range(16)]
        PW = a(8, 2, 8)
        PWN = a(8, 8)
        B1, B2 = a(2, P + T), a(2, P + T)
        VT1 = a(T)
        UY = a(2, T)
        HSC = WK[:, :, :].rearrange("p a (b n t) -> p (a b) n t", b=2, n=2)
        HF = AR[:, m_at:m_at + KD * T].rearrange("p (k t) -> p k t", k=KD)
        MIX_HI2 = rounded(seg_at, 8, T)
        MIX_LO = rounded(mix_at, 8, T)
        with nc.Block() as block:
            @block.sync
            def _(sp):
                stream(sp, base, SLOTS, V_XQ + SLOTS)

            @block.gpsimd
            def _(pool):
                for t in (XP, XD, B1, B2):
                    pool.memset(t, 0.0).then_inc(S("cleared"), 1)

            @block.tensor
            def _(pe):
                norm_sum(pe, SQ, KD, "m")
                pe.wait_ge(S("h_low"), KD)
                tiles = Tiles()

                S5_AFTER = (3, 4, 6, 11, 15, 20)

                def s5_input(j):
                    if j >= 2:
                        pe.wait_ge(S("bu_taken"), j - 1)
                    for n in range(2):
                        mm = pe.matmul(PS[:, 6 + j % 2, n * T:(n + 1) * T], SB[:, n, j, :], ZU[:, j // 4, :],
                                       start=True, stop=True)
                    mm.then_inc(S("bu"), 1)

                def s5_output(j):
                    pe.wait_ge(S("scanned"), j + 1)
                    for n in range(2):
                        mm = pe.matmul(PS[:, 1 - j // 4, 0:T], SCM[:, n, j, :], HSC[:, j % 4, n, :],
                                       start=(j % 4 == 0 and n == 0), stop=(j % 4 == 3 and n == 1))
                    mm.then_inc(S("s5_y"), 1)

                i = 0
                pe.wait_ge(S("small"), 80)
                for j, after in enumerate(S5_AFTER):
                    tiles.linear(pe, base, V_IN + i, after - i, H_HI, H_LO, i)
                    i = after
                    pe.wait_ge(S("bank_emptied"), 1 + j // 4)
                    s5_input(j)
                tiles.linear(pe, base, V_IN + i, N_IN2 - i, H_HI, H_LO, i)
                b = tiles.bank(pe)
                for tt in range(TT):
                    for k in range(KD):
                        mm = pe.matmul(PS[:, b, tt * 12:tt * 12 + 12], HF[:, k, tt * P:(tt + 1) * P], WDT[:, k, :],
                                       start=(k == 0), stop=(k == KD - 1))
                mm.then_inc(S("dt_raw"), 1)
                s5_input(6)
                for j in range(4):
                    s5_output(j)
                pe.wait_ge(S("da"), 1)
                b = tiles.bank(pe)
                for c in range(TT):
                    pe.matmul(PS[:, b, c * 12:c * 12 + 12], tri, DA[:, c, :], start=True, stop=True)
                    mm = pe.matmul(PS[:, b, 24 + c * 12:36 + c * 12], ones, DA[:, c, :], start=True, stop=True)
                mm.then_inc(S("cumulated"), 1)
                for c in range(TT):
                    for n in range(3):
                        b = tiles.bank(pe)
                        for m in range(4):
                            h = 4 * n + m
                            mm = pe.matmul(PS[:, b, m * P:(m + 1) * P],
                                           DA[:, c, h:h + 1].to_broadcast([P, P]), tri, start=True, stop=True)
                        mm.then_inc(S("rows"), 1)
                s5_input(7)
                pe.wait_ge(S("xbc"), 14)
                for g in range(4):
                    b = tiles.bank(pe)
                    pe.matmul(PS[:, b, 0:T], XC[:, 6 + g, 0:P], XC[:, 10 + g, :], start=True, stop=True)
                    pe.matmul(PS[:, b, T:384], XC[:, 6 + g, P:T], XC[:, 10 + g, P:T], start=True, stop=True)\
                        .then_inc(S("cb"), 1)
                for s in range(TT):
                    for n, m in ((0, 4), (4, 2)):
                        b = tiles.bank(pe)
                        for i in range(m):
                            mm = pe.transpose(PS[:, b, i * P:(i + 1) * P], XC[:, n + i, s * P:(s + 1) * P], ident)
                        mm.then_inc(S("x_turned"), 1)
                for j in (4, 5, 6):
                    s5_output(j)
                pe.wait_ge(S("bank_emptied"), tiles.n)
                pe.wait_ge(S("decayed"), 14)
                for i in range(6):
                    b = tiles.bank(pe)
                    for n, h in enumerate((2 * i, 2 * i + 1)):
                        pe.matmul(PS[:, b, 0:T], XD[:, 0, h, :], M[:, h, 0:T], start=(n == 0), stop=False,
                                  skip_group_check=True)
                        mm = pe.matmul(PS[:, b, P:T], XD[:, 1, h, :], M[:, h, T:384], start=False, stop=(n == 1),
                                       skip_group_check=True)
                    mm.then_inc(S("ssd_y"), 1)
                s5_output(7)
                at["ssd_y"] = tiles.n
                pe.wait_ge(S("ssd_squares"), 1)
                for k in range(6):
                    mm = pe.matmul(PS[:, 7, 0:T], ones, SYQ[:, k, :], start=(k == 0), stop=(k == 5))
                mm.then_inc(S("ssd_sum"), 1)
                pe.wait_ge(S("s5_gelu"), 1)
                for f in range(2):
                    b = tiles.bank(pe)
                    for k in range(2):
                        mm = pe.matmul(PS[:, b, 0:T], GLU[:, k, f * P:(f + 1) * P], UY[:, k, :],
                                       start=(k == 0), stop=(k == 1))
                    mm.then_inc(S("glu"), 1)
                pe.wait_ge(S("mix_low"), 3)
                tiles.linear(pe, base, V_OUT, 8, MIX_HI2, MIX_LO, N_IN2)

            @block.scalar
            def _(sc):
                act = Steps(sc, S)
                for t, src in ((V2, vec2), (SB, s5b), (SCM, s5c), (GLU, wglu), (WDT, wdt)):
                    sc.dma_start(t, src).then_inc(S("small"), 16)
                act.wait("small", 80)
                act(sc.activation(C8[0], V2[:, W_DT:W_DT + 8], ACT.Exp), "s5_dt")
                norm_squares(act, X[:, :, :], SQ, "m")
                act.wait("angle", 10)
                act(sc.activation(C8[4], C8[4], ACT.Sin), "s5_cos")
                act(sc.activation(C8[3], C8[3], ACT.Sin), "s5_sin")
                act(sc.activation(C8[5], C8[5], ACT.Exp), "s5_mag")
                norm_root(act, "m")
                for i in range(HIGHS):
                    split_high(act, base, V_IN + i, True)
                operand_high(act, H_HI, H, KD, "m_applied", "h_high")
                act(sc.activation(HF, H[:, :, :], ACT.Copy), "h_kept")
                nxt = Drain(sc)
                act.wait("cleared", 4)
                for i in range(N_IN2):
                    sc.wait_ge(units_used, used(base, V_IN + i))
                    dst = ZU[:, i, :] if i < 8 else XP[:, i - 8, 3:3 + T]
                    act.mark(sc.activation(dst, PS[:, nxt(), 0:T], ACT.Copy), "bank_emptied")
                    split_high(act, base, V_IN + i + HIGHS, False)
                act.wait("dt_abs", 1)
                act(sc.activation(S3, S2, ACT.Exp, scale=-1.0), "dt_exp")
                act(sc.activation(NEGA, V2[:, W_ALOG:W_ALOG + 12], ACT.Exp), "a_exp")
                act.wait("dt_one", 1)
                act(sc.activation(S4, S4, ACT.Ln), "dt_ln")
                act.wait("decay_in", 1)
                act(sc.activation(DEC, DEC, ACT.Exp), "decay_exp")
                for n in range(6):
                    act.wait("rows", n + 1)
                    if n >= 3:
                        b = 2 + (N_IN2 + 2 + n) % 4
                        act(sc.activation(ER1[:, 4 * (n - 3):4 * (n - 2), :].rearrange("p a b -> p (a b)"),
                                          PS[:, b, :], ACT.Exp), "rows_exp")
                act.wait("bank_emptied", N_IN2 + 2 + 6)
                act.wait("segs", 18)
                act(sc.activation(SEG, SEG, ACT.Exp), "seg_exp")
                for i in range(14):
                    act.wait("convolved", i + 1)
                    act.mark(sc.activation(XC[:, i, :], XC[:, i, :], ACT.Silu,
                                           bias=V2[:, W_CB + i:W_CB + i + 1]), "xbc")
                act(sc.activation(ZU[:, 2:8, :], ZU[:, 2:8, :], ACT.Silu), "z_silu")
                act.wait("gated_y", 6)
                act(sc.activation(SYQ, MIX[:, 2:8, :], ACT.Square), "ssd_squares")
                act.wait("skipped", 2)
                act(sc.activation(UY, UY, ACT.Gelu_apprx_tanh), "s5_gelu")
                act.wait("ssd_inverse", 1)
                act(sc.activation(RS[:, 2, :], RS[:, 1, :], ACT.Sqrt), "ssd_rstd")
                act.wait("bank_emptied", at["ssd_y"])
                for f in range(2):
                    act.wait("glu", f + 1)
                    act.mark(sc.activation(MIX[:, f, :], PS[:, 2 + (at["ssd_y"] + f) % 4, 0:T], ACT.Sigmoid),
                             "bank_emptied")
                act.wait("mixed", 8)
                act(sc.activation(MIX_HI2[:, 0:2, :], MIX[:, 0:2, :], ACT.Copy), "mix_high")
                for i in range(HIGHS, 8):
                    split_high(act, base, V_OUT + i, False)

            @block.vector
            def _(dve):
                v = Steps(dve, S)
                v.wait("small", 80)
                LRr, LIi = C8[1], V2[:, W_LI:W_LI + 8]
                v(dve.tensor_scalar(LRr, V2[:, W_LR:W_LR + 8], -1e-4, None, ALU.min), "s5")
                v.wait("s5_dt", 1)
                tt_ = lambda o, x, y, op: v(dve.tensor_tensor(o, x, y, op), "s5")
                th, red, red2, mag, t0 = C8[2], C8[3], C8[4], C8[5], C8[6]
                tt_(th, LIi, C8[0], ALU.mult)
                tt_(mag, LRr, C8[0], ALU.mult)
                reduce_angle(v, red, th, t0)
                quarter_turn(v, red2, red, t0)
                norm_inverse(v, D, "m")
                for i in range(HIGHS):
                    split_low(v, V_IN + i, i)
                norm_apply(v, H[:, :, :], X[:, :, :], V2[:, W_MIX:W_MIX + 8], None, "m")
                v.wait("h_kept", 1)
                operand_low(v, H_LO, H, H_HI, KD, "h_high", "h_low")
                v.wait("s5_mag", 1)
                are, aim, den, am1, fre, fim = C8[8], C8[9], C8[10], C8[11], C8[12], C8[13]
                tt_(are, mag, red2, ALU.mult)
                tt_(aim, mag, red, ALU.mult)
                tt_(den, LRr, LRr, ALU.mult)
                tt_(t0, LIi, LIi, ALU.mult)
                tt_(den, den, t0, ALU.add)
                v(dve.tensor_scalar(am1, are, -1.0, None, ALU.add), "s5")
                tt_(fre, am1, LRr, ALU.mult)
                tt_(t0, aim, LIi, ALU.mult)
                tt_(fre, fre, t0, ALU.add)
                v(dve.reciprocal(den, den), "s5")
                tt_(fre, fre, den, ALU.mult)
                tt_(fim, aim, LRr, ALU.mult)
                tt_(t0, am1, LIi, ALU.mult)
                tt_(fim, fim, t0, ALU.subtract)
                tt_(fim, fim, den, ALU.mult)
                nfre, nfim = C8[14], C8[15]
                v(dve.tensor_scalar(nfre, fre, -1.0, None, ALU.mult), "s5")
                v(dve.tensor_scalar(nfim, fim, -1.0, None, ALU.mult), "s5")
                v(dve.tensor_copy(PW[:, 0, 0, :], are), "s5")
                v(dve.tensor_scalar(PW[:, 0, 1, :], aim, -1.0, None, ALU.mult), "s5")
                for k in range(7):
                    r0, i0 = PW[:, k, 0, :], PW[:, k, 1, :]
                    tt_(PW[:, k + 1, 0, :], r0, r0, ALU.mult)
                    tt_(t0, i0, i0, ALU.mult)
                    tt_(PW[:, k + 1, 0, :], PW[:, k + 1, 0, :], t0, ALU.subtract)
                    tt_(t0, r0, i0, ALU.mult)
                    v(dve.tensor_scalar(PW[:, k + 1, 1, :], t0, 2.0, None, ALU.mult), "s5")
                v(dve.tensor_scalar(PWN, PW[:, :, 1, :], -1.0, None, ALU.mult), "s5")

                def scan(n0, n1):
                    for j, step in (divmod(n, 9) for n in range(n0, n1)):
                        if step == 0:
                            fr, fi, nfr, nfi = (t[:, j:j + 1] for t in (fre, fim, nfre, nfim))
                            v.wait("bu", j + 1)
                            vre, vim = PS[:, 6 + j % 2, 0:T], PS[:, 6 + j % 2, T:2 * T]
                            v(dve.tensor_scalar(VT1, vim, fi, None, ALU.mult), "s5")
                            v(dve.scalar_tensor_tensor(B1[:, 0, P:], vre, fr, VT1, ALU.mult, ALU.subtract), "s5")
                            v(dve.tensor_scalar(VT1, vre, nfi, None, ALU.mult), "s5")
                            v(dve.scalar_tensor_tensor(B1[:, 1, P:], vim, nfr, VT1, ALU.mult, ALU.add), "bu_taken")
                            continue
                        k = step - 1
                        o = P - 2 ** k
                        final = k == 7
                        src, dst = (B1, B2) if k % 2 == 0 else (B2, B1)
                        if final and j >= 4:
                            v.wait("s5_y", j - 3)
                        both = HSC[:, j % 4, :, :] if final else dst[:, :, P:]
                        pr, pi, pn = PW[:, k, 0, j:j + 1], PW[:, k, 1, j:j + 1], PWN[:, k, j:j + 1]
                        v(dve.scalar_tensor_tensor(both, src[:, :, o:o + T], pr, src[:, :, P:], ALU.mult, ALU.add), "s5")
                        v.mark(dve.scalar_tensor_tensor(both[:, 0, :], src[:, 1, o:o + T], pn, both[:, 0, :],
                                                        ALU.mult, ALU.add), "s5")
                        v(dve.scalar_tensor_tensor(both[:, 1, :], src[:, 0, o:o + T], pi, both[:, 1, :],
                                                   ALU.mult, ALU.add), "scanned" if final else "s5")

                v.wait("cleared", 4)
                for i in range(N_IN2):
                    split_low(v, V_IN + i + HIGHS, i + HIGHS)
                    if i >= 3:
                        scan(2 * (i - 3), 2 * (i - 3) + 2)
                nxt = Drain(dve)
                nxt.n = N_IN2
                scan(38, 40)
                v.wait("dt_raw", 1)
                v.n["bank_emptied"] = N_IN2
                v.wait("bank_emptied", N_IN2)
                raw = S1.rearrange("p (a b) -> p a b", a=2)
                v(dve.tensor_tensor(raw, PS[:, nxt(), 0:24].rearrange("p (a b) -> p a b", a=2),
                                    V2[:, W_DTB:W_DTB + 12].unsqueeze(1).to_broadcast([P, 2, 12]), ALU.add),
                  "bank_emptied")
                v(dve.tensor_scalar(S2, S1, -1.0, None, ALU.mult), "dt")
                v(dve.tensor_tensor(S2, S2, S1, ALU.max), "dt_abs")
                scan(40, 43)
                v.wait("dt_exp", 1)
                v(dve.tensor_scalar(S4, S3, 1.0, None, ALU.add), "dt")
                v(dve.tensor_scalar(S2, S4, -1.0, None, ALU.add), "dt_one")
                scan(43, 45)
                v.wait("dt_ln", 1)
                W1 = DTM.rearrange("p a b -> p (a b)")
                v(dve.tensor_scalar(W1, S2, 0.0, None, ALU.is_equal), "dt")
                v(dve.tensor_tensor(S2, S2, W1, ALU.add), "dt")
                v(dve.tensor_tensor(S4, S4, W1, ALU.add), "dt")
                v(dve.reciprocal(S2, S2), "dt")
                v(dve.tensor_tensor(S4, S4, S2, ALU.mult), "dt")
                v(dve.tensor_tensor(S4, S4, S3, ALU.mult), "dt")
                v(dve.scalar_tensor_tensor(W1, S1, 0.0, S4, ALU.max, ALU.add), "dt")
                v.wait("a_exp", 1)
                v(dve.tensor_scalar(NEGA, NEGA, -1.0, None, ALU.mult), "dt")
                v(dve.tensor_tensor(DA, DTM, NEGA.unsqueeze(1).to_broadcast([P, 2, 12]), ALU.mult), "da")
                scan(45, 50)
                v.wait("cumulated", 1)
                b = nxt()
                v(dve.tensor_copy(ACS, PS[:, b, 0:24].rearrange("p (a b) -> p a b", a=2)), "dt")
                v(dve.tensor_copy(LAST, PS[:, b, 24:48].rearrange("p (a b) -> p a b", a=2)), "bank_emptied")
                v(dve.tensor_tensor(DEC, LAST[:, 0, :], ACS[:, 0, :], ALU.subtract), "decay_in")
                scan(50, 54)
                for n in range(6):
                    v.wait("rows", n + 1)
                    b = nxt()
                    c = n // 3
                    if c == 1:
                        v.wait("rows_exp", n - 2)
                    for m in range(4):
                        h = 4 * (n % 3) + m
                        v.mark(dve.scalar_tensor_tensor(SEG[:, c, h, :], PS[:, b, m * P:(m + 1) * P],
                                                        ACS[:, c, h:h + 1], causal, ALU.subtract, ALU.add),
                               "segs" if m < 3 else "bank_emptied")
                v.wait("bank_emptied", nxt.n)
                for i in range(14):
                    for n in range(4):
                        w = V2[:, W_CW + 14 * n + i:W_CW + 14 * n + i + 1]
                        if n == 0:
                            v(dve.tensor_scalar(XC[:, i, :], XP[:, i, 0:T], w, None, ALU.mult), "conv")
                        else:
                            v(dve.scalar_tensor_tensor(XC[:, i, :], XP[:, i, n:n + T], w, XC[:, i, :],
                                                       ALU.mult, ALU.add), "convolved" if n == 3 else "conv")
                scan(54, 63)
                for g in range(4):
                    v.wait("cb", g + 1)
                    v(dve.tensor_copy(CB[:, g, :], PS[:, nxt(), 0:384]), "bank_emptied")
                v.wait("seg_exp", 1)
                for g in range(4):
                    hs = slice(3 * g, 3 * g + 3)
                    for c, o in ((0, 0), (1, T)):
                        v.mark(dve.tensor_tensor(M[:, hs, o:o + P], SEG[:, c, hs, :],
                                                 CB[:, g:g + 1, o:o + P].to_broadcast([P, 3, P]), ALU.mult), "decayed")
                v.wait("decay_exp", 1)
                for h in range(12):
                    i = dve.scalar_tensor_tensor(M[:, h, P:T], CB[:, h // 3, P:T], DEC[:, h:h + 1], ER1[:, h, :],
                                                 ALU.mult, ALU.mult)
                    if h % 2:
                        v.mark(i, "decayed")
                for s in range(TT):
                    for n, m in ((0, 4), (4, 2)):
                        v.wait("x_turned", 2 * s + n // 4 + 1)
                        b = nxt()
                        src = PS[:, b, 0:m * P].rearrange("p (i h d) -> p i h d", i=m, h=2)
                        for q in range(2):
                            hsl = slice(2 * n + q, 2 * (n + m) + q - 1, 2)
                            i = dve.tensor_tensor(XD[:, s, hsl, 64 * q:64 * q + 64], src[:, :, q, :],
                                                  DTM[:, s, hsl].unsqueeze(2).to_broadcast([P, m, 64]), ALU.mult)
                            v.mark(i, "x_dt" if q == 0 else "bank_emptied")
                scan(63, 72)
                v.wait("z_silu", 1)
                for i in range(6):
                    v.wait("ssd_y", i + 1)
                    v(dve.scalar_tensor_tensor(MIX[:, 2 + i, :], XC[:, i, :], V2[:, W_SD + i:W_SD + i + 1],
                                               PS[:, nxt(), 0:T], ALU.mult, ALU.add), "bank_emptied")
                    v(dve.tensor_tensor(MIX[:, 2 + i, :], MIX[:, 2 + i, :], ZU[:, 2 + i, :], ALU.mult), "gated_y")
                for f in range(2):
                    v.wait("s5_y", 4 * f + 4)
                    v(dve.scalar_tensor_tensor(UY[:, f, :], ZU[:, f, :], V2[:, W_UD + f:W_UD + f + 1],
                                               PS[:, 1 - f, 0:T], ALU.mult, ALU.add), "skipped")
                norm_inverse(v, 6 * P, "ssd", bank=7)
                v.wait("ssd_rstd", 1)
                for i in range(6):
                    v(dve.scalar_tensor_tensor(MIX[:, 2 + i, :], MIX[:, 2 + i, :], V2[:, W_SN + i:W_SN + i + 1],
                                               RS[:, 2, :], ALU.mult, ALU.mult), "mixed")
                v.wait("mixed", 6)
                v.mark(dve.tensor_copy(MIX_HI2[:, 2:8, :], MIX[:, 2:8, :]), "mix_low")
                v.wait("mix_low", 1)
                v.mark(dve.tensor_tensor(MIX_LO[:, 2:8, :], MIX[:, 2:8, :], MIX_HI2[:, 2:8, :].bitcast(F32),
                                         ALU.subtract), "mix_low")
                v.wait("bank_emptied", at["ssd_y"] + 2)
                for f in range(2):
                    nxt()
                    v.mark(dve.tensor_tensor(MIX[:, f, :], MIX[:, f, :], UY[:, f, :], ALU.mult), "mixed")
                v.n["bank_emptied"] = nxt.n
                v.wait("mix_high", 1)
                v.mark(dve.tensor_tensor(MIX_LO[:, 0:2, :], MIX[:, 0:2, :], MIX_HI2[:, 0:2, :].bitcast(F32),
                                         ALU.subtract), "mix_low")
                for i in range(8):
                    if i + HIGHS < 8:
                        split_low(v, V_OUT + i + HIGHS, N_IN2 + i + HIGHS)
                    dve.wait_ge(units_used, used(base, V_OUT + i))
                    v.mark(dve.tensor_tensor(X[:, i, :], PS[:, nxt(), 0:T], X[:, i, :], ALU.add), "bank_emptied")
                v.wait("bank_emptied", nxt.n)
        end_of_block()

        a = Arena()
        a.at = keep
        MEM = a(8, T)
        MN, MN_LO, MN_HI = a.split(8, T)
        SQ, SQ2 = a(8, T), a(8, T)
        QX, KX = a(8, T), a(8, T)
        OX, OX_LO, OX_HI = a.split(8, T)
        VX = a(2, D)
        EX = a(8, T)
        MX, NMX, SUM = a(8), a(8), a(8)
        PTX = a(4, 2, T)
        with nc.Block() as block:
            @block.sync
            def _(sp):
                sp.dma_start(MEM, memT).then_inc(S("mem"), 16)
                stream(sp, base, V_XQ + SLOTS, V_FFN + SLOTS)

            @block.tensor
            def _(pe):
                norm_sum(pe, SQ, KD, "xa")
                pe.wait_ge(S("xa_rstd"), 1)
                norm_sum(pe, SQ2, KD, "mem", bank=0)
                pe.wait_ge(S("h_low"), KD)
                tiles = Tiles()
                tiles.linear(pe, base, V_XQ, 8, H_HI, H_LO, 0)
                pe.wait_ge(S("mem_low"), KD)
                tiles.linear(pe, base, V_XK, 8, MN_HI, MN_LO, 8)
                pe.wait_ge(S("bank_emptied"), 16)
                for k in range(KD):
                    pe.wait_ge(S("split"), 16 + k + 1)
                    w_hi, w_lo = parts_of(V_XV + k)
                    for mt in range(TT):
                        m = slice(mt * P, (mt + 1) * P)
                        for n in range(2):
                            o, dst = slice(n * 512, (n + 1) * 512), PS[:, 4 + 2 * mt + n, :]
                            pe.matmul(dst, MN_HI[:, k, m], w_hi[:, o], start=(k == 0), stop=False)
                            pe.matmul(dst, MN_HI[:, k, m], w_lo[:, o], start=False, stop=False)
                            mm = pe.matmul(dst, MN_LO[:, k, m], w_hi[:, o], start=False, stop=(k == KD - 1))
                    mm.then_inc(units_used, 1)
                for h in range(4):
                    if h >= 2:
                        pe.wait_ge(S("exps"), 2 * (h - 1))
                    for qt in range(TT):
                        for k in range(2):
                            mm = pe.matmul(PS[:, h % 2, qt * T:(qt + 1) * T], QX[:, 2 * h + k, qt * P:(qt + 1) * P],
                                           KX[:, 2 * h + k, :], start=(k == 0), stop=(k == 1))
                    mm.then_inc(S("scored"), 1)
                pe.wait_ge(S("values"), 4)
                for h in range(4):
                    pe.wait_ge(S("probs"), h + 1)
                    b = tiles.bank(pe)
                    for mt in range(TT):
                        for qt in range(TT):
                            mm = pe.transpose(PS[:, b, mt * T + qt * P:mt * T + (qt + 1) * P],
                                              EX[:, 2 * h + qt, mt * P:(mt + 1) * P], ident)
                    mm.then_inc(S("probs_turned"), 1)
                for c in range(8):
                    b = tiles.bank(pe)
                    pe.wait_ge(S("bank_emptied"), 16 + c // 2 + 1)
                    for mt in range(TT):
                        mm = pe.matmul(PS[:, b, 0:T], VX[:, mt, c * P:(c + 1) * P], PTX[:, c // 2, mt, :],
                                       start=(mt == 0), stop=(mt == 1))
                    mm.then_inc(S("attended"), 1)
                pe.wait_ge(S("o_low"), 8)
                tiles.linear(pe, base, V_XO, 8, OX_HI, OX_LO, 24)

            @block.scalar
            def _(sc):
                act = Steps(sc, S)
                norm_squares(act, X[:, :, :], SQ, "xa")
                act.wait("mem", 16)
                norm_squares(act, MEM, SQ2, "mem")
                norm_root(act, "xa")
                for i in range(HIGHS):
                    split_high(act, base, V_XQ + i, True)
                operand_high(act, H_HI, H, KD, "xa_applied", "h_high")
                norm_root(act, "mem")
                operand_high(act, MN_HI, MN, KD, "mem_applied", "mem_high")
                nxt = Drain(sc)
                for i in range(16):
                    sc.wait_ge(units_used, used(base, V_XQ + i))
                    dst = QX[:, i, :] if i < 8 else KX[:, i - 8, :]
                    act.mark(sc.activation(dst, PS[:, nxt(), 0:T], ACT.Copy), "bank_emptied")
                    split_high(act, base, V_XQ + i + HIGHS, False)
                for k in range(HIGHS, 8 + HIGHS):
                    split_high(act, base, V_XV + k, False)
                sc.wait_ge(units_used, used(base, V_XV + 7))
                for n in range(4):
                    act.mark(sc.activation(VX[:, n // 2, (n % 2) * 512:(n % 2 + 1) * 512], PS[:, 4 + n, :], ACT.Copy),
                             "values")
                for h in range(4):
                    act.wait("maxed", h + 1)
                    for qt in range(TT):
                        i = 2 * h + qt
                        act.mark(sc.activation(EX[:, i, :], PS[:, h % 2, qt * T:(qt + 1) * T], ACT.Exp,
                                               bias=NMX[:, i:i + 1], scale=1.0 / 16, accum_out=SUM[:, i:i + 1]), "exps")
                for c in range(8):
                    act.wait("bank_emptied", 20 + c + 1)
                    act.mark(sc.activation(OX_HI[:, c, :], OX[:, c, :], ACT.Copy), "o_high")
                for k in range(HIGHS, 8):
                    split_high(act, base, V_XO + k, False)

            @block.vector
            def _(dve):
                v = Steps(dve, S)
                norm_inverse(v, D, "xa")
                for i in range(HIGHS):
                    split_low(v, V_XQ + i, i)
                norm_apply(v, H[:, :, :], X[:, :, :], V2[:, W_XA:W_XA + 8], None, "xa")
                operand_low(v, H_LO, H, H_HI, KD, "h_high", "h_low")
                norm_inverse(v, D, "mem", bank=0)
                norm_apply(v, MN, MEM, V2[:, W_MEM:W_MEM + 8], None, "mem")
                operand_low(v, MN_LO, MN, MN_HI, KD, "mem_high", "mem_low")
                for i in range(24):
                    split_low(v, V_XQ + i + HIGHS, i + HIGHS)
                for h in range(4):
                    v.wait("scored", h + 1)
                    v(dve.tensor_reduce(MX[:, 2 * h:2 * h + 2], PS[:, h % 2, :].rearrange("p (a b) -> p a b", a=2),
                                        AX_X, ALU.max), "max")
                    v(dve.tensor_scalar(NMX[:, 2 * h:2 * h + 2], MX[:, 2 * h:2 * h + 2], -1.0 / 16, None, ALU.mult),
                      "maxed")
                for h in range(4):
                    v.wait("exps", 2 * h + 2)
                    v(dve.reciprocal(SUM[:, 2 * h:2 * h + 2], SUM[:, 2 * h:2 * h + 2]), "inverse")
                    v(dve.tensor_tensor(EX[:, 2 * h:2 * h + 2, :], EX[:, 2 * h:2 * h + 2, :],
                                        SUM[:, 2 * h:2 * h + 2].unsqueeze(2).to_broadcast([P, 2, T]), ALU.mult), "probs")
                nxt = Drain(dve)
                nxt.n = 16
                v.n["bank_emptied"] = 16
                for h in range(4):
                    v.wait("probs_turned", h + 1)
                    v(dve.tensor_copy(PTX[:, h, :, :].rearrange("p a b -> p (a b)"), PS[:, nxt(), :]), "bank_emptied")
                for c in range(8):
                    v.wait("attended", c + 1)
                    v(dve.tensor_copy(OX[:, c, :], PS[:, nxt(), 0:T]), "bank_emptied")
                operand_low(v, OX_LO, OX, OX_HI, 8, "o_high", "o_low")
                for i in range(8):
                    if i + HIGHS < 8:
                        split_low(v, V_XO + i + HIGHS, 24 + i + HIGHS)
                    dve.wait_ge(units_used, used(base, V_XO + i))
                    v.mark(dve.tensor_tensor(X[:, i, :], PS[:, nxt(), 0:T], X[:, i, :], ALU.add), "bank_emptied")
                v.wait("bank_emptied", nxt.n)
        end_of_block()

        a = Arena()
        a.at = keep
        SQ = a(KD, T)
        GP = a(2, T + 2)
        CV = a(2, T)
        F, F_LO, F_HI = a.split(2, T)
        with nc.Block() as block:
            @block.sync
            def _(sp):
                stream(sp, base, V_FFN + SLOTS, UNITS2)
                sp.wait_ge(S("final_applied"), KD)
                sp.dma_start(out, H[:, :, :]).then_inc(S("stored"), 16)
                sp.wait_ge(S("stored"), 16)

            @block.gpsimd
            def _(pool):
                pool.memset(GP, 0.0).then_inc(S("cleared"), 1)

            @block.tensor
            def _(pe):
                norm_sum(pe, SQ, KD, "ff")
                pe.wait_ge(S("h_low"), KD)
                u = V_FFN

                def up(f, u):
                    if f >= 2:
                        pe.wait_ge(S("hidden"), f - 1)
                    for n in range(2):
                        pe.wait_ge(S("split"), u + n - V_FFN + 1)
                        unit_product(pe, PS[:, 2 + f % 2, n * T:(n + 1) * T], u + n, H_HI, H_LO)\
                            .then_inc(units_used, 1)
                    return u + 2

                def down(f, u):
                    pe.wait_ge(S("hidden_low"), f + 1)
                    pe.wait_ge(S("split"), u - V_FFN + 1)
                    unit_spread(pe, u, F_HI[:, f % 2, :], F_LO[:, f % 2, :], f == 0, f == N_FF - 1)\
                        .then_inc(units_used, 1)
                    return u + 1

                u = up(0, u)
                for f in range(1, N_FF):
                    u = up(f, u)
                    u = down(f - 1, u)
                u = down(N_FF - 1, u)
                assert u == UNITS2
                norm_sum(pe, SQ, KD, "final")

            @block.scalar
            def _(sc):
                act = Steps(sc, S)
                norm_squares(act, X[:, :, :], SQ, "ff")
                norm_root(act, "ff")
                act.wait("cleared", 1)
                for i in range(HIGHS):
                    split_high(act, base, V_FFN + i, True)
                operand_high(act, H_HI, H, KD, "ff_applied", "h_high")
                for f in range(N_FF):
                    sc.wait_ge(units_used, used(base, V_FFN + (1 if f == 0 else 3 * f)))
                    if f >= 2:
                        act.wait("convolved", f - 1)
                    act.mark(sc.activation(GP[:, f % 2, 2:2 + T], PS[:, 2 + f % 2, 0:T], ACT.Copy), "g_copied")
                    act.wait("convolved", f + 1)
                    act(sc.activation(CV[:, f % 2, :], CV[:, f % 2, :], ACT.Silu,
                                      bias=V2[:, W_FB + f:W_FB + f + 1]), "silu")
                    if 3 * f + 4 < 3 * N_FF:
                        split_high(act, base, V_FFN + 3 * f + 4, False)
                    act.wait("hidden", f + 1)
                    act.mark(sc.activation(F_HI[:, f % 2, :], F[:, f % 2, :], ACT.Copy), "hidden_high")
                    for i in (5, 6):
                        if 3 * f + i < 3 * N_FF:
                            split_high(act, base, V_FFN + 3 * f + i, False)
                act.wait("x_done", KD)
                norm_squares(act, X[:, :, :], SQ, "final")
                norm_root(act, "final")

            @block.vector
            def _(dve):
                v = Steps(dve, S)
                norm_inverse(v, D, "ff")
                for i in range(HIGHS):
                    split_low(v, V_FFN + i, i)
                norm_apply(v, H[:, :, :], X[:, :, :], V2[:, W_FFN:W_FFN + 8], None, "ff")
                operand_low(v, H_LO, H, H_HI, KD, "h_high", "h_low")
                for f in range(N_FF):
                    s = f % 2
                    v.wait("g_copied", f + 1)
                    for n in range(3):
                        w = V2[:, W_FW + N_FF * n + f:W_FW + N_FF * n + f + 1]
                        if n == 0:
                            v(dve.tensor_scalar(CV[:, s, :], GP[:, s, 0:T], w, None, ALU.mult), "conv")
                        else:
                            v(dve.scalar_tensor_tensor(CV[:, s, :], GP[:, s, n:n + T], w, CV[:, s, :],
                                                       ALU.mult, ALU.add), "convolved" if n == 2 else "conv")
                    v.wait("silu", f + 1)
                    if f >= 2:
                        dve.wait_ge(units_used, used(base, V_FFN + 3 * (f - 2) + 4))
                    v(dve.tensor_tensor(F[:, s, :], CV[:, s, :], PS[:, 2 + s, T:2 * T], ALU.mult), "hidden")
                    if 3 * f + 4 < 3 * N_FF:
                        split_low(v, V_FFN + 3 * f + 4, 3 * f + 4)
                    v.wait("hidden_high", f + 1)
                    v.mark(dve.tensor_tensor(F_LO[:, s, :], F[:, s, :], F_HI[:, s, :].bitcast(F32), ALU.subtract),
                           "hidden_low")
                    for i in (5, 6):
                        if 3 * f + i < 3 * N_FF:
                            split_low(v, V_FFN + 3 * f + i, 3 * f + i)
                dve.wait_ge(units_used, used(base, UNITS2 - 1))
                for k in range(KD):
                    v.mark(dve.tensor_tensor(X[:, k, :], PS[:, 4 + k // 2, (k % 2) * T:(k % 2 + 1) * T],
                                             X[:, k, :], ALU.add), "x_done")
                norm_inverse(v, D, "final")
                norm_apply(v, H[:, :, :], X[:, :, :], V2[:, W_FIN:W_FIN + 8], None, "final")


def tables():
    import numpy as np

    c = np.zeros((P, C_COLS), np.float32)
    i = np.arange(P)
    c[:, C_ID:C_ID + P] = np.eye(P)
    c[:, C_ONE:C_ONE + P] = 1.0
    c[:, C_BLK:C_BLK + P] = i[:, None] // 64 == i[None] // 64
    r = np.zeros((P, P), np.float32)
    for h in (0, 64):
        for m in range(8):
            r[h + m + 8, h + m] = -1.0
            r[h + m, h + m + 8] = 1.0
    c[:, C_ROT:C_ROT + P] = r
    c[:, C_TRI:C_TRI + P] = i[:, None] <= i[None]
    c[:, C_CAUS:C_CAUS + P] = np.where(i[:, None] <= i[None], 0.0, NEG)
    t = np.arange(T)
    m = np.zeros((P, D), np.float32)
    for qt in range(TT):
        far = np.abs((i + qt * P)[:, None] - t[None]) > 128
        m[:, C_MASK + qt * T:C_MASK + (qt + 1) * T] = np.where(far, NEG, 0.0)
    for g, w in enumerate((2, 4, 8, 16)):
        n = np.clip(t + w // 2, 0, T) - np.clip(t - w // 2, 0, T)
        m[64 * (g % 2):64 * (g % 2) + 64, C_CNT + (g // 2) * T:C_CNT + (g // 2 + 1) * T] = 1.0 / n
    c[:, C_IOTA:C_IOTA + P] = i
    c[:, C_I16:C_I16 + 16] = np.arange(16)
    inv = np.float32(500000.0) ** (-np.arange(0, 16, 2, dtype=np.float32) / np.float32(16))
    for h in (0, 8, 64, 72):
        c[h:h + 8, C_INV] = inv
    return c, m


def kernel(**inputs):
    import numpy as np
    import concourse.bacc as bacc
    from concourse.bass_utils import run_bass_kernel_spmd as run

    g = {k: np.asarray(v) for k, v in inputs.items()}

    def tiles(w):
        k, n = w.shape
        return w.reshape(k // P, P, n // P, P).transpose(2, 1, 0, 3).reshape(n // P, P, k)

    def by_part(x):
        return x.reshape(-1, P).T

    ws = np.zeros((UNITS, P, D), np.float32)
    heads = [j + 4 * half for j in range(4) for half in range(2)]
    perm = np.concatenate([np.arange(64) + 64 * h for h in heads])
    for l in range(DEPTH):
        b = l * PER_LAYER
        pv = ws[b]
        pv[:, L_N1:L_N1 + 8] = by_part(g["norm1_g"][l])
        pv[:, L_N2:L_N2 + 8] = by_part(g["norm2_g"][l])
        pv[:, L_BADA:L_BADA + 48] = by_part(g["b_ada"][l])
        pv[:, L_QG] = np.tile(g["q_norm_g"][l], 2)
        pv[:, L_KG] = np.tile(g["k_norm_g"][l], 2)
        for n in range(3):
            pv[:, L_CONV + 2 * n:L_CONV + 2 * n + 2] = by_part(g["conv_w"][l, n])
        pv[:, L_PSC:L_PSC + 2] = by_part(g["pool_scale"][l])
        pv[:, L_SINK:L_SINK + 16] = np.repeat(g["attn_sink"][l][heads], 2)[None]
        for n in range(4):
            r = 64 * (n % 2)
            ws[b + 1, r:r + 64, (n // 2) * P + r:(n // 2) * P + r + 64] = g["pool_w"][l, n]
        for n in range(2):
            ws[b + 1, :, T + n * P:T + (n + 1) * P] = g["peer_keys"][l, n].T
        ada = g["w_ada"][l].T.reshape(N_ADA + N_ADB, P, D)
        ws[b + U_ADA:b + U_ADA + N_ADA] = ada[:N_ADA]
        ws[b + U_ADB:b + U_ADB + N_ADB] = ada[N_ADA:]
        w_in = g["w_in"][l]
        ws[b + U_IN:b + U_IN + N_IN] = tiles(np.concatenate([w_in[:, :512][:, perm], w_in[:, 512:]], 1))
        w_out = g["w_out"][l]
        ws[b + U_OUT:b + U_OUT + N_OUT] = tiles(np.concatenate([w_out[:512][perm], w_out[512:]], 0))
        ws[b + U_WQ:b + U_WQ + N_WQ] = tiles(g["peer_wq"][l])
        eu = g["peer_u"][l].reshape(P, P, KD, P).transpose(1, 3, 2, 0).reshape(P, P, D)
        ev = g["peer_v"][l].reshape(P, P, D).transpose(1, 0, 2)
        e = ws[b + U_EXP:b + PER_LAYER]
        e[0:2] = eu[0:2]
        mid = e[2:254].reshape(63, 4, P, D)
        mid[:, 0:2] = eu[2:].reshape(63, 2, P, D)
        mid[:, 2:4] = ev[:126].reshape(63, 2, P, D)
        e[254:256] = ev[126:128]
    s = ws[BASE2:]
    w_in2 = g["w_in_2"][0]
    s[V_IN:V_IN + N_IN2] = tiles(np.ascontiguousarray(w_in2[:, :N_IN2 * P]))
    wdt = w_in2[:, N_IN2 * P:].reshape(KD, P, 12).transpose(1, 0, 2)
    s[V_OUT:V_OUT + 8] = tiles(g["w_out_2"][0])
    s[V_XQ:V_XQ + 8] = tiles(g["xa_wq_2"][0])
    s[V_XK:V_XK + 8] = tiles(g["xa_wk_2"][0])
    s[V_XV:V_XV + 8] = g["xa_wv_2"][0].reshape(KD, P, D)
    s[V_XO:V_XO + 8] = tiles(g["xa_wo_2"][0])
    up = tiles(g["ffn_w_up_2"][0])
    dn = g["ffn_w_down_2"][0].reshape(N_FF, P, D)
    f = s[V_FFN:]
    f[0], f[1] = up[0], up[N_FF]
    mid = f[2:65].reshape(N_FF - 1, 3, P, D)
    mid[:, 0], mid[:, 1], mid[:, 2] = up[1:N_FF], up[N_FF + 1:], dn[:N_FF - 1]
    f[65] = dn[N_FF - 1]

    v2 = np.zeros((P, W_COLS), np.float32)

    def put(at, x):
        v2[:, at:at + x.shape[1]] = x

    for at, name in ((W_MIX, "mix_norm_w_2"), (W_XA, "xa_norm_w_2"), (W_MEM, "mem_norm_w_2"),
                     (W_FFN, "ffn_norm_w_2"), (W_SN, "ssd_norm_w_2"), (W_CB, "ssd_conv_b_2"),
                     (W_UD, "s5_d_2"), (W_FB, "ffn_conv_b_2")):
        put(at, by_part(g[name][0]))
    put(W_FIN, by_part(g["final_norm_w_2"]))
    put(W_CW, by_part(g["ssd_conv_w_2"][0]))
    put(W_FW, by_part(g["ffn_conv_w_2"][0]))
    put(W_SD, by_part(np.repeat(g["ssd_d_2"][0], 64)))
    put(W_LR, by_part(g["s5_lambda_re_2"][0].reshape(-1)))
    put(W_LI, by_part(g["s5_lambda_im_2"][0].reshape(-1)))
    put(W_DT, by_part(np.repeat(g["s5_log_dt_2"][0], 64)))
    put(W_DTB, np.repeat(g["ssd_dt_bias_2"][0][None], P, 0))
    put(W_ALOG, np.repeat(g["ssd_a_log_2"][0][None], P, 0))
    s5b = np.zeros((P, 2, 8, P), np.float32)
    s5c = np.zeros((P, 2, 8, P), np.float32)
    for n, part in enumerate(("re", "im")):
        for j in range(8):
            for q in range(2):
                grp = 2 * j + q
                r = 16 * (grp % 8)
                s5b[r:r + 16, n, j, 64 * q:64 * q + 64] = g[f"s5_b_{part}_2"][0, grp].T
                s5c[64 * q:64 * q + 64, n, j, r:r + 16] = g[f"s5_c_{part}_2"][0, grp].T

    def fm(x):
        return np.ascontiguousarray(x[0].T.reshape(KD, P, T).transpose(1, 0, 2))

    consts, mixconst = tables()
    arrays = {
        "wstream": ws, "consts": consts, "mixconst": mixconst, "crow": np.repeat(g["c"], P, 0),
        "xT": fm(g["x"]), "memT": fm(g["mem_2"]),
        "pos": np.ascontiguousarray(np.repeat(g["positions"], P, 0)),
        "vec2": v2, "s5b": s5b, "s5c": s5c,
        "wglu": np.ascontiguousarray(g["s5_w_glu_2"][0].reshape(2, P, T).transpose(1, 0, 2)),
        "wdt": np.ascontiguousarray(wdt),
    }
    nc = bacc.Bacc("TRN2", target_bir_lowering=False, num_devices=1, dynamic_dma_scratch_size=1024)
    args = [nc.dram_tensor(k, a.shape, mybir.dt.from_np(a.dtype), kind="ExternalInput").ap()
            for k, a in arrays.items()]
    args.append(nc.dram_tensor("outT", (P, KD, T), F32, kind="ExternalOutput").ap())
    program(nc, *args)
    r = run(nc, [arrays], core_ids=[0])
    return np.ascontiguousarray(r.results[0]["outT"].transpose(2, 1, 0).reshape(1, T, D))
```
